# Optimizing a Trainium2 kernel written in Bass

```python
import jax, jax.numpy as jnp
from jax import lax
import numpy as np
import math
import jax
import jax.numpy as jnp

D_MODEL = 1024
BATCH = 1
SEQ = 256
DEPTH = 2

HEAD_DIM = 64
N_TOK_HEADS = 12
N_KV_HEADS = 3
GQA_GROUP = N_TOK_HEADS // N_KV_HEADS
N_MEM_HEADS = 4
N_MEM = 256
Q_W = N_TOK_HEADS * HEAD_DIM
KV_W = N_KV_HEADS * HEAD_DIM
QM_W = N_MEM_HEADS * HEAD_DIM
IN_W = Q_W + 2 * KV_W + QM_W
MIX_WIDTH = Q_W + QM_W
D_FF = -(-8 * D_MODEL // (3 * 256)) * 256
N_MIXERS = 3
BLOCK = 128
A_RADIUS = 128
C_GROUPS = ((128, 1), (512, 4), (2048, 16))
ROPE_THETA = 500000.0
ROPE_DIMS = HEAD_DIM // 4
AXIAL_THETA = 10000.0
GRID_W = 64
EPS = 1e-6
N_A = (DEPTH + 2) // N_MIXERS
N_B = (DEPTH + 1) // N_MIXERS
ATTN_SCALE = HEAD_DIM ** -0.5


def rms_norm(x, g):
    xf = x.astype(jnp.float32)
    y = xf * lax.rsqrt(jnp.mean(xf * xf, axis=-1, keepdims=True) + EPS)
    return (y * g.astype(jnp.float32)).astype(x.dtype)

def rope_table(pos, n_dims, theta):
    inv = theta ** (-(jnp.arange(0, n_dims, 2, dtype=jnp.float32) / n_dims))
    ang = pos.astype(jnp.float32)[:, None] * inv[None, :]
    return jnp.cos(ang), jnp.sin(ang)

def apply_rotary(x, cos, sin):
    half = x.shape[-1] // 2
    xf = x.astype(jnp.float32)
    x1, x2 = xf[..., :half], xf[..., half:]
    c, s = cos[:, None, :], sin[:, None, :]
    return jnp.concatenate([x1 * c - x2 * s, x2 * c + x1 * s], axis=-1).astype(x.dtype)

def partial_rope(x, cos, sin):
    return jnp.concatenate([apply_rotary(x[..., :ROPE_DIMS], cos, sin), x[..., ROPE_DIMS:]], axis=-1)

def axial_rope(x, cos_r, sin_r, cos_c, sin_c):
    half = HEAD_DIM // 2
    return jnp.concatenate([apply_rotary(x[..., :half], cos_r, sin_r),
                            apply_rotary(x[..., half:], cos_c, sin_c)], axis=-1)

def banded_attention(q, k, v, radius, sink=None):
    B, L, KVH, G, HD = q.shape
    blk = radius
    nb = -(-L // blk)
    Lp = nb * blk
    pad = Lp - L
    qb = jnp.pad(q, [(0, 0), (0, pad), (0, 0), (0, 0), (0, 0)]).reshape(B, nb, blk, KVH, G, HD)

    def windows(t):
        tp = jnp.pad(t, [(0, 0), (blk, blk + pad), (0, 0), (0, 0)]).reshape(B, nb + 2, blk, KVH, HD)
        return jnp.concatenate([tp[:, :-2], tp[:, 1:-1], tp[:, 2:]], axis=2)

    kw, vw = windows(k), windows(v)
    qpos = jnp.arange(Lp).reshape(nb, blk)
    kpos = (jnp.arange(nb)[:, None] - 1) * blk + jnp.arange(3 * blk)[None, :]
    mask = ((jnp.abs(qpos[:, :, None] - kpos[:, None, :]) <= radius)
            & (kpos >= 0)[:, None, :] & (kpos < L)[:, None, :])
    s = jnp.einsum('bnqhgd,bnkhd->bnhgqk', qb, kw, preferred_element_type=jnp.float32) * ATTN_SCALE
    s = jnp.where(mask[None, :, None, None], s, -jnp.inf)
    m = jnp.max(s, axis=-1, keepdims=True)
    if sink is not None:
        sk = sink.astype(jnp.float32)[None, None, :, :, None, None]
        m = jnp.maximum(m, sk)
    p = jnp.exp(s - m)
    denom = jnp.sum(p, axis=-1)
    if sink is not None:
        denom = denom + jnp.exp(sk - m)[..., 0]
    o = jnp.einsum('bnhgqk,bnkhd->bnqhgd', p.astype(v.dtype), vw)
    den_t = jnp.transpose(denom, (0, 1, 4, 2, 3))
    o = (o / den_t[..., None]).astype(q.dtype).reshape(B, Lp, KVH, G, HD)[:, :L]
    lse = jnp.transpose(m[..., 0] + jnp.log(denom), (0, 1, 4, 2, 3)).reshape(B, Lp, KVH, G)[:, :L]
    return o, lse

def full_attention_blocks(q, k, v):
    B, S, KVH, G, HD = q.shape
    nb = S // BLOCK
    qb = jnp.moveaxis(q.reshape(B, nb, BLOCK, KVH, G, HD), 1, 0)

    def one_block(qblk):
        s = jnp.einsum('bqhgd,bkhd->bhgqk', qblk, k, preferred_element_type=jnp.float32) * ATTN_SCALE
        p = jax.nn.softmax(s, axis=-1)
        return jnp.einsum('bhgqk,bkhd->bqhgd', p.astype(v.dtype), v)

    o = lax.map(one_block, qb)
    return jnp.moveaxis(o, 0, 1).reshape(B, S, KVH, G, HD)

def mixer_a(q, k, v, sink, cos_p, sin_p):
    B, S = q.shape[:2]
    q = partial_rope(q, cos_p, sin_p).reshape(B, S, N_KV_HEADS, GQA_GROUP, HEAD_DIM)
    k = partial_rope(k, cos_p, sin_p)
    o, _ = banded_attention(q, k, v, A_RADIUS, sink.reshape(N_KV_HEADS, GQA_GROUP))
    return o.reshape(B, S, Q_W)

def mixer_b(q, k, v, qk_g, cos_r, sin_r, cos_c, sin_c):
    B, S = q.shape[:2]
    q = axial_rope(rms_norm(q, qk_g[0]), cos_r, sin_r, cos_c, sin_c)
    k = axial_rope(rms_norm(k, qk_g[1]), cos_r, sin_r, cos_c, sin_c)
    o = full_attention_blocks(q.reshape(B, S, N_KV_HEADS, GQA_GROUP, HEAD_DIM), k, v)
    return o.reshape(B, S, Q_W)

def dilated_group(q, k, v, dil, radius):
    B, S = q.shape[:2]
    L = S // dil

    def split(t):
        t = jnp.moveaxis(t.reshape((B, L, dil) + t.shape[2:]), 2, 1)
        return t.reshape((B * dil, L) + t.shape[3:])

    def merge(t):
        t = jnp.moveaxis(t.reshape((B, dil, L) + t.shape[2:]), 1, 2)
        return t.reshape((B, S) + t.shape[3:])

    o, lse = banded_attention(split(q)[:, :, None], split(k)[:, :, None], split(v)[:, :, None], radius)
    return merge(o[:, :, 0]), merge(lse[:, :, 0])

def mixer_c(q, k, v, cos_p, sin_p):
    B, S = q.shape[:2]
    q = partial_rope(q, cos_p, sin_p)
    k = partial_rope(k, cos_p, sin_p)
    outs, lses = [], []
    for g, (window, dil) in enumerate(C_GROUPS):
        o, l = dilated_group(q[:, :, g * GQA_GROUP:(g + 1) * GQA_GROUP], k[:, :, g], v[:, :, g],
                             dil, window // (2 * dil))
        outs.append(o)
        lses.append(l)
    alpha = jax.nn.softmax(jnp.stack(lses, axis=2), axis=2)
    o = jnp.stack(outs, axis=2) * alpha[..., None].astype(q.dtype)
    return o.reshape(B, S, Q_W)

def memory_attention(qm, km, vm):
    s = jnp.einsum('bshd,bmhd->bhsm', qm, km, preferred_element_type=jnp.float32) * ATTN_SCALE
    p = jax.nn.softmax(s, axis=-1)
    o = jnp.einsum('bhsm,bmhd->bshd', p.astype(vm.dtype), vm)
    return o.reshape(qm.shape[0], qm.shape[1], QM_W)

def first_inputs(seed: int = 0) -> dict:
    key = jax.random.key(seed)
    ks = jax.random.split(key, 14)
    nrm = jax.random.normal
    f32 = jnp.float32
    return {
        'x': nrm(ks[0], (BATCH, SEQ, D_MODEL), f32),
        'mem': nrm(ks[1], (BATCH, N_MEM, D_MODEL), f32),
        'mem_norm_g': 1.0 + 0.02 * nrm(ks[2], (D_MODEL,), f32),
        'w_in': nrm(ks[3], (DEPTH, D_MODEL, IN_W), f32) * D_MODEL ** -0.5,
        'w_mem_kv': nrm(ks[4], (DEPTH, D_MODEL, 2 * QM_W), f32) * D_MODEL ** -0.5,
        'w_o': nrm(ks[5], (DEPTH, MIX_WIDTH, D_MODEL), f32) * MIX_WIDTH ** -0.5,
        'g_mix_pre': 1.0 + 0.02 * nrm(ks[6], (DEPTH, D_MODEL), f32),
        'g_mix_post': 1.0 + 0.02 * nrm(ks[7], (DEPTH, D_MODEL), f32),
        'attn_sink': 0.5 * nrm(ks[8], (N_A, N_TOK_HEADS), f32),
        'qk_norm_g': 1.0 + 0.02 * nrm(ks[9], (N_B, 2, HEAD_DIM), f32),
        'w_gate_up': nrm(ks[10], (DEPTH, D_MODEL, 2 * D_FF), f32) * D_MODEL ** -0.5,
        'w_down': nrm(ks[11], (DEPTH, D_FF, D_MODEL), f32) * D_FF ** -0.5,
        'g_ffn_pre': 1.0 + 0.02 * nrm(ks[12], (DEPTH, D_MODEL), f32),
        'g_ffn_post': 1.0 + 0.02 * nrm(ks[13], (DEPTH, D_MODEL), f32),
    }

def first_block(x, mem, mem_norm_g, w_in, w_mem_kv, w_o, g_mix_pre, g_mix_post, attn_sink,
              qk_norm_g, w_gate_up, w_down, g_ffn_pre, g_ffn_post):
    B, S, _ = x.shape
    rows = S // GRID_W
    pos = jnp.arange(S, dtype=jnp.int32)
    row_ids = jnp.repeat(jnp.arange(rows, dtype=jnp.int32), GRID_W)
    col_ids = jnp.tile(jnp.arange(GRID_W, dtype=jnp.int32), rows)
    cos_p, sin_p = rope_table(pos, ROPE_DIMS, ROPE_THETA)
    cos_r, sin_r = rope_table(row_ids, HEAD_DIM // 2, AXIAL_THETA)
    cos_c, sin_c = rope_table(col_ids, HEAD_DIM // 2, AXIAL_THETA)
    mem_n = rms_norm(mem, mem_norm_g)

    for i in range(DEPTH):
        h = rms_norm(x, g_mix_pre[i])
        proj = h @ w_in[i]
        q = proj[..., :Q_W].reshape(B, S, N_TOK_HEADS, HEAD_DIM)
        k = proj[..., Q_W:Q_W + KV_W].reshape(B, S, N_KV_HEADS, HEAD_DIM)
        v = proj[..., Q_W + KV_W:Q_W + 2 * KV_W].reshape(B, S, N_KV_HEADS, HEAD_DIM)
        qm = proj[..., Q_W + 2 * KV_W:].reshape(B, S, N_MEM_HEADS, HEAD_DIM)
        kind = i % N_MIXERS
        if kind == 0:
            tok = mixer_a(q, k, v, attn_sink[i // N_MIXERS], cos_p, sin_p)
        elif kind == 1:
            tok = mixer_b(q, k, v, qk_norm_g[i // N_MIXERS], cos_r, sin_r, cos_c, sin_c)
        else:
            tok = mixer_c(q, k, v, cos_p, sin_p)
        mkv = mem_n @ w_mem_kv[i]
        km = mkv[..., :QM_W].reshape(B, N_MEM, N_MEM_HEADS, HEAD_DIM)
        vm = mkv[..., QM_W:].reshape(B, N_MEM, N_MEM_HEADS, HEAD_DIM)
        mo = memory_attention(qm, km, vm)
        o = jnp.concatenate([tok, mo], axis=-1) @ w_o[i]
        x = x + rms_norm(o, g_mix_post[i])

        h = rms_norm(x, g_ffn_pre[i])
        gu = h @ w_gate_up[i]
        f = (jax.nn.silu(gu[..., :D_FF]) * gu[..., D_FF:]) @ w_down[i]
        x = x + rms_norm(f, g_ffn_post[i])
    return x


Q_BLOCK = 128
D_FF_2 = 2816
NEG_BIG = -1e30
FORCE_SCORE = 1e9

A_HEADS = 6
A_Q_RANK = 192
A_KV_RANK = 128
A_NOPE = 64
A_ROPE = 32
A_V = 64

B_HEADS = 6
B_KV_GROUPS = 2
B_HPG = B_HEADS // B_KV_GROUPS
B_DH = 64
B_ROT = B_DH // 4
CMP_LEN = 32
CMP_STRIDE = 16
SLC_LEN = 64
SLC_TOPN = 16
WINDOW = 512

C_HEADS = 4
C_DH = 32
C_ROT = C_DH // 4

MIX_WIDTH_2 = A_HEADS * A_V + B_HEADS * B_DH + C_HEADS * 2 * C_DH
A_COLS = A_Q_RANK + A_KV_RANK + A_ROPE
B_COLS = B_HEADS * B_DH + 6 * B_KV_GROUPS * B_DH + 3 * B_HEADS
C_COLS = 3 * C_HEADS * 2 * C_DH
IN_COLS = A_COLS + B_COLS + C_COLS


def rmsnorm(x, g):
    xf = x.astype(jnp.float32)
    y = xf * lax.rsqrt(jnp.mean(xf * xf, axis=-1, keepdims=True) + EPS)
    return (y * g.astype(jnp.float32)).astype(x.dtype)

def rope_tables(positions, rot_dim):
    inv_freq = 1.0 / (ROPE_THETA ** (jnp.arange(0, rot_dim, 2, dtype=jnp.float32) / rot_dim))
    ang = positions.astype(jnp.float32)[..., None] * inv_freq
    return (jnp.cos(ang), jnp.sin(ang))

def apply_rope(x, cs):
    cos, sin = cs
    B, T, r2 = cos.shape
    shape = (B,) + (1,) * (x.ndim - 3) + (T, r2)
    cos = cos.reshape(shape)
    sin = sin.reshape(shape)
    xf = x.astype(jnp.float32)
    x1, x2 = xf[..., :r2], xf[..., r2:]
    return jnp.concatenate([x1 * cos - x2 * sin, x1 * sin + x2 * cos], axis=-1).astype(x.dtype)

def partial_rope_2(x, cs):
    r = 2 * cs[0].shape[-1]
    return jnp.concatenate([apply_rope(x[..., :r], cs), x[..., r:]], axis=-1)

def swiglu(x, wg, wu, wd):
    return (jax.nn.silu(x @ wg) * (x @ wu)) @ wd

def causal_block_attention(q, k, v, scale):
    B, H, T, dk = q.shape
    nb = T // Q_BLOCK
    q_blocks = jnp.moveaxis(q.reshape(B, H, nb, Q_BLOCK, dk), 2, 0)
    kpos = jnp.arange(T)

    def one_block(args):
        qi, i = args
        s = jnp.einsum('bhqd,bhkd->bhqk', qi, k, preferred_element_type=jnp.float32) * scale
        qpos = i * Q_BLOCK + jnp.arange(Q_BLOCK)
        s = jnp.where(kpos[None, :] <= qpos[:, None], s, -jnp.inf)
        p = jax.nn.softmax(s, axis=-1)
        return jnp.einsum('bhqk,bhkd->bhqd', p.astype(v.dtype), v)

    o = lax.map(one_block, (q_blocks, jnp.arange(nb)))
    return jnp.moveaxis(o, 0, 2).reshape(B, H, T, v.shape[-1])

def mla_mixer(h, cs_a, q_norm, kv_norm, w_uq, w_ukv):
    B, T, _ = h.shape
    c_q, c_kv, k_pe = jnp.split(h, [A_Q_RANK, A_Q_RANK + A_KV_RANK], axis=-1)
    q = (rmsnorm(c_q, q_norm) @ w_uq).reshape(B, T, A_HEADS, A_NOPE + A_ROPE).transpose(0, 2, 1, 3)
    kv = (rmsnorm(c_kv, kv_norm) @ w_ukv).reshape(B, T, A_HEADS, A_NOPE + A_V).transpose(0, 2, 1, 3)
    q = jnp.concatenate([q[..., :A_NOPE], apply_rope(q[..., A_NOPE:], cs_a)], axis=-1)
    k_pe = apply_rope(k_pe[:, None], cs_a)
    k = jnp.concatenate([kv[..., :A_NOPE], jnp.broadcast_to(k_pe, (B, A_HEADS, T, A_ROPE))], axis=-1)
    v = kv[..., A_NOPE:]
    o = causal_block_attention(q, k, v, (A_NOPE + A_ROPE) ** -0.5)
    return o.transpose(0, 2, 1, 3).reshape(B, T, A_HEADS * A_V)

def nsa_mixer(h, cs_b, pe_k, pe_v, phi_k1, phi_k2, phi_v1, phi_v2):
    B, T, _ = h.shape
    G, Hg, DH = B_KV_GROUPS, B_HPG, B_DH
    qw, kvw = B_HEADS * DH, G * DH
    offs = [qw + j * kvw for j in range(7)]
    q, kc, vc, ks, vs, kw, vw, gate_logits = jnp.split(h, offs, axis=-1)

    def split_kv(t):
        return t.reshape(B, T, G, DH).transpose(0, 2, 1, 3)

    q = partial_rope_2(q.reshape(B, T, G, Hg, DH).transpose(0, 2, 3, 1, 4), cs_b)
    kc, ks, kw = [partial_rope_2(split_kv(t), cs_b) for t in (kc, ks, kw)]
    vc, vs, vw = [split_kv(t) for t in (vc, vs, vw)]
    scale = DH ** -0.5
    tpos = jnp.arange(T)
    nb = T // Q_BLOCK

    n_cmp = (T - CMP_LEN) // CMP_STRIDE + 1
    cmp_idx = jnp.arange(n_cmp)[:, None] * CMP_STRIDE + jnp.arange(CMP_LEN)[None, :]

    def compress(t, pe, w1, w2):
        blk = (t[:, :, cmp_idx] + pe).reshape(B, G, n_cmp, CMP_LEN * DH)
        return jax.nn.silu(blk @ w1) @ w2

    k_cmp = compress(kc, pe_k, phi_k1, phi_k2)
    v_cmp = compress(vc, pe_v, phi_v1, phi_v2)
    s_cmp = jnp.einsum('bghtd,bgcd->bghtc', q, k_cmp, preferred_element_type=jnp.float32) * scale
    cmp_mask = cmp_idx[:, -1][None, :] <= tpos[:, None]
    p_cmp = jax.nn.softmax(jnp.where(cmp_mask, s_cmp, NEG_BIG), axis=-1) * cmp_mask
    o_cmp = jnp.einsum('bghtc,bgcd->bghtd', p_cmp.astype(v_cmp.dtype), v_cmp)

    n_slc = T // SLC_LEN
    top_n = min(SLC_TOPN, n_slc)
    blk_start = jnp.arange(n_slc) * SLC_LEN
    overlap = ((cmp_idx[:, 0][:, None] < blk_start[None, :] + SLC_LEN)
               & (cmp_idx[:, -1][:, None] >= blk_start[None, :])).astype(jnp.float32)
    imp = jnp.einsum('bghtc,cm->bgtm', p_cmp, overlap)
    cur = (tpos // SLC_LEN)[:, None]
    m = jnp.arange(n_slc)[None, :]
    forced = (m == 0) | (m == cur) | (m == cur - 1)
    score = jnp.where(forced, FORCE_SCORE, jnp.where(m <= cur, imp, -1.0))
    sel = lax.top_k(score, top_n)[1]

    ks_blk = ks.reshape(B, G, n_slc, SLC_LEN, DH)
    vs_blk = vs.reshape(B, G, n_slc, SLC_LEN, DH)
    q_blocks = jnp.moveaxis(q.reshape(B, G, Hg, nb, Q_BLOCK, DH), 3, 0)
    sel_blocks = jnp.moveaxis(sel.reshape(B, G, nb, Q_BLOCK, top_n), 2, 0)
    gather_blocks = jax.vmap(jax.vmap(lambda blocks, ids: blocks[ids]))

    def slc_block(args):
        qi, si, i = args
        kg = gather_blocks(ks_blk, si).reshape(B, G, Q_BLOCK, top_n * SLC_LEN, DH)
        vg = gather_blocks(vs_blk, si).reshape(B, G, Q_BLOCK, top_n * SLC_LEN, DH)
        kpos = (si[..., None] * SLC_LEN + jnp.arange(SLC_LEN)).reshape(B, G, Q_BLOCK, top_n * SLC_LEN)
        qpos = i * Q_BLOCK + jnp.arange(Q_BLOCK)
        valid = kpos <= qpos[:, None]
        s = jnp.einsum('bghqd,bgqkd->bghqk', qi, kg, preferred_element_type=jnp.float32) * scale
        p = jax.nn.softmax(jnp.where(valid[:, :, None], s, -jnp.inf), axis=-1)
        return jnp.einsum('bghqk,bgqkd->bghqd', p.astype(vg.dtype), vg)

    o_slc = lax.map(slc_block, (q_blocks, sel_blocks, jnp.arange(nb)))
    o_slc = jnp.moveaxis(o_slc, 0, 3).reshape(B, G, Hg, T, DH)

    kw_pad = jnp.pad(kw, ((0, 0), (0, 0), (WINDOW, 0), (0, 0)))
    vw_pad = jnp.pad(vw, ((0, 0), (0, 0), (WINDOW, 0), (0, 0)))
    band = jnp.arange(nb)[:, None] * Q_BLOCK + jnp.arange(WINDOW + Q_BLOCK)[None, :]
    kband = kw_pad[:, :, band]
    vband = vw_pad[:, :, band]
    kpos_w = band - WINDOW
    qpos_w = tpos.reshape(nb, Q_BLOCK)
    dist = qpos_w[:, :, None] - kpos_w[:, None, :]
    wmask = (dist >= 0) & (dist < WINDOW) & (kpos_w[:, None, :] >= 0)
    qwb = q.reshape(B, G, Hg, nb, Q_BLOCK, DH)
    s_w = jnp.einsum('bghnqd,bgnkd->bghnqk', qwb, kband, preferred_element_type=jnp.float32) * scale
    p_w = jax.nn.softmax(jnp.where(wmask, s_w, -jnp.inf), axis=-1)
    o_win = jnp.einsum('bghnqk,bgnkd->bghnqd', p_w.astype(vband.dtype), vband).reshape(B, G, Hg, T, DH)

    g = jax.nn.sigmoid(gate_logits.astype(jnp.float32)).reshape(B, T, G, Hg, 3)
    g = g.transpose(0, 2, 3, 1, 4).astype(q.dtype)
    o = g[..., 0:1] * o_cmp + g[..., 1:2] * o_slc + g[..., 2:3] * o_win
    return o.transpose(0, 3, 1, 2, 4).reshape(B, T, B_HEADS * DH)

def diff_mixer(h, cs_c, lq1, lk1, lq2, lk2, sub_norm, layer_idx):
    B, T, _ = h.shape
    q, k, v = jnp.split(h, 3, axis=-1)
    q = partial_rope_2(q.reshape(B, T, C_HEADS, 2, C_DH).transpose(0, 2, 3, 1, 4), cs_c)
    k = partial_rope_2(k.reshape(B, T, C_HEADS, 2, C_DH).transpose(0, 2, 3, 1, 4), cs_c)
    v = v.reshape(B, T, C_HEADS, 2 * C_DH).transpose(0, 2, 1, 3)
    lam_init = 0.8 - 0.6 * math.exp(-0.3 * layer_idx)
    f32 = jnp.float32
    lam = (jnp.exp(jnp.sum(lq1.astype(f32) * lk1.astype(f32)))
           - jnp.exp(jnp.sum(lq2.astype(f32) * lk2.astype(f32))) + lam_init)
    scale = C_DH ** -0.5
    o1 = causal_block_attention(q[:, :, 0], k[:, :, 0], v, scale)
    o2 = causal_block_attention(q[:, :, 1], k[:, :, 1], v, scale)
    o = o1.astype(f32) - lam * o2.astype(f32)
    o = (rmsnorm(o, sub_norm) * (1.0 - lam_init)).astype(h.dtype)
    return o.transpose(0, 2, 1, 3).reshape(B, T, C_HEADS * 2 * C_DH)

def second_inputs(seed: int = 0) -> dict:
    key = jax.random.key(seed)
    keys = iter(jax.random.split(key, 40))
    f32 = jnp.float32
    L = DEPTH

    def nrm(shape, fan_in):
        return jax.random.normal(next(keys), shape, f32) * (fan_in ** -0.5)

    def gain(shape):
        return 1.0 + 0.02 * jax.random.normal(next(keys), shape, f32)

    def small(shape, s):
        return s * jax.random.normal(next(keys), shape, f32)

    x = jax.random.normal(next(keys), (BATCH, SEQ, D_MODEL), f32)
    offset = jax.random.randint(next(keys), (BATCH, 1), 0, 1024, dtype=jnp.int32)
    positions = offset + jnp.arange(SEQ, dtype=jnp.int32)[None, :]
    return {
        'x': x,
        'positions': positions,
        'ffn1_norm': gain((L, D_MODEL)),
        'ffn1_wg': nrm((L, D_MODEL, D_FF_2), D_MODEL),
        'ffn1_wu': nrm((L, D_MODEL, D_FF_2), D_MODEL),
        'ffn1_wd': nrm((L, D_FF_2, D_MODEL), D_FF_2),
        'mix_norm': gain((L, D_MODEL)),
        'w_in': nrm((L, D_MODEL, IN_COLS), D_MODEL),
        'mla_q_norm': gain((L, A_Q_RANK)),
        'mla_kv_norm': gain((L, A_KV_RANK)),
        'mla_w_uq': nrm((L, A_Q_RANK, A_HEADS * (A_NOPE + A_ROPE)), A_Q_RANK),
        'mla_w_ukv': nrm((L, A_KV_RANK, A_HEADS * (A_NOPE + A_V)), A_KV_RANK),
        'nsa_pe_k': small((L, CMP_LEN, B_DH), 0.1),
        'nsa_pe_v': small((L, CMP_LEN, B_DH), 0.1),
        'nsa_phi_k1': nrm((L, CMP_LEN * B_DH, B_DH), CMP_LEN * B_DH),
        'nsa_phi_k2': nrm((L, B_DH, B_DH), B_DH),
        'nsa_phi_v1': nrm((L, CMP_LEN * B_DH, B_DH), CMP_LEN * B_DH),
        'nsa_phi_v2': nrm((L, B_DH, B_DH), B_DH),
        'diff_lq1': small((L, C_DH), 0.1),
        'diff_lk1': small((L, C_DH), 0.1),
        'diff_lq2': small((L, C_DH), 0.1),
        'diff_lk2': small((L, C_DH), 0.1),
        'diff_sub_norm': gain((L, 2 * C_DH)),
        'w_out': nrm((L, MIX_WIDTH_2, D_MODEL), MIX_WIDTH_2),
        'ffn2_norm': gain((L, D_MODEL)),
        'ffn2_wg': nrm((L, D_MODEL, D_FF_2), D_MODEL),
        'ffn2_wu': nrm((L, D_MODEL, D_FF_2), D_MODEL),
        'ffn2_wd': nrm((L, D_FF_2, D_MODEL), D_FF_2),
        'final_norm': gain((D_MODEL,)),
    }

def second_block(x, positions, ffn1_norm, ffn1_wg, ffn1_wu, ffn1_wd, mix_norm, w_in,
              mla_q_norm, mla_kv_norm, mla_w_uq, mla_w_ukv,
              nsa_pe_k, nsa_pe_v, nsa_phi_k1, nsa_phi_k2, nsa_phi_v1, nsa_phi_v2,
              diff_lq1, diff_lk1, diff_lq2, diff_lk2, diff_sub_norm, w_out,
              ffn2_norm, ffn2_wg, ffn2_wu, ffn2_wd, final_norm):
    cs_a = rope_tables(positions, A_ROPE)
    cs_b = rope_tables(positions, B_ROT)
    cs_c = rope_tables(positions, C_ROT)
    for l in range(DEPTH):
        x = x + 0.5 * swiglu(rmsnorm(x, ffn1_norm[l]), ffn1_wg[l], ffn1_wu[l], ffn1_wd[l])
        h = rmsnorm(x, mix_norm[l]) @ w_in[l]
        h_a, h_b, h_c = jnp.split(h, [A_COLS, A_COLS + B_COLS], axis=-1)
        o_a = mla_mixer(h_a, cs_a, mla_q_norm[l], mla_kv_norm[l], mla_w_uq[l], mla_w_ukv[l])
        o_b = nsa_mixer(h_b, cs_b, nsa_pe_k[l], nsa_pe_v[l], nsa_phi_k1[l], nsa_phi_k2[l],
                        nsa_phi_v1[l], nsa_phi_v2[l])
        o_c = diff_mixer(h_c, cs_c, diff_lq1[l], diff_lk1[l], diff_lq2[l], diff_lk2[l],
                         diff_sub_norm[l], l)
        o = jnp.concatenate([o_a, o_b, o_c], axis=-1)
        x = x + o @ w_out[l]
        x = x + 0.5 * swiglu(rmsnorm(x, ffn2_norm[l]), ffn2_wg[l], ffn2_wu[l], ffn2_wd[l])
    return rmsnorm(x, final_norm)


def setup_inputs(seed=0):
    out = dict(first_inputs(seed))
    for name, value in second_inputs(seed + 1).items():
        if name != "x":
            out[name + "_2"] = value
    return out


def reference(
    x, mem, mem_norm_g, w_in, w_mem_kv, w_o, g_mix_pre, g_mix_post, attn_sink, qk_norm_g,
    w_gate_up, w_down, g_ffn_pre, g_ffn_post, positions_2, ffn1_norm_2, ffn1_wg_2, ffn1_wu_2,
    ffn1_wd_2, mix_norm_2, w_in_2, mla_q_norm_2, mla_kv_norm_2, mla_w_uq_2, mla_w_ukv_2,
    nsa_pe_k_2, nsa_pe_v_2, nsa_phi_k1_2, nsa_phi_k2_2, nsa_phi_v1_2, nsa_phi_v2_2, diff_lq1_2,
    diff_lk1_2, diff_lq2_2, diff_lk2_2, diff_sub_norm_2, w_out_2, ffn2_norm_2, ffn2_wg_2,
    ffn2_wu_2, ffn2_wd_2, final_norm_2,
):
    x = first_block(
        x, mem, mem_norm_g, w_in, w_mem_kv, w_o, g_mix_pre, g_mix_post, attn_sink, qk_norm_g,
        w_gate_up, w_down, g_ffn_pre, g_ffn_post,
    )
    return second_block(
        x, positions_2, ffn1_norm_2, ffn1_wg_2, ffn1_wu_2, ffn1_wd_2, mix_norm_2, w_in_2,
        mla_q_norm_2, mla_kv_norm_2, mla_w_uq_2, mla_w_ukv_2, nsa_pe_k_2, nsa_pe_v_2,
        nsa_phi_k1_2, nsa_phi_k2_2, nsa_phi_v1_2, nsa_phi_v2_2, diff_lq1_2, diff_lk1_2,
        diff_lq2_2, diff_lk2_2, diff_sub_norm_2, w_out_2, ffn2_norm_2, ffn2_wg_2, ffn2_wu_2,
        ffn2_wd_2, final_norm_2,
    )


_drawn_inputs = setup_inputs


def setup_inputs(seed=0):
    import zlib

    import numpy as np

    out = dict(_drawn_inputs(seed))
    spreads = {}
    factors = {'mem_norm_g': 4.317,
     'attn_sink': 8.0,
     'qk_norm_g': 8.0,
     'g_ffn_pre': 2.711,
     'g_ffn_post': 3.699,
     'ffn1_norm_2': 8.0,
     'mix_norm_2': 7.398,
     'mla_q_norm_2': 8.0,
     'mla_kv_norm_2': 8.0,
     'nsa_pe_k_2': 8.0,
     'nsa_pe_v_2': 6.298,
     'nsa_phi_k1_2': 4.716,
     'nsa_phi_k2_2': 4.316,
     'diff_lq1_2': 8.0,
     'diff_lk1_2': 8.0,
     'diff_lq2_2': 8.0,
     'diff_lk2_2': 8.0,
     'diff_sub_norm_2': 55.524,
     'ffn2_norm_2': 8.0,
     'final_norm_2': 8.262}
    for name, (base, spread) in spreads.items():
        noise = np.random.default_rng([zlib.crc32(name.encode()), seed]).standard_normal(out[name].shape)
        drawn = base * np.exp(spread * noise) if base else spread * noise
        out[name] = jnp.asarray(drawn.astype(out[name].dtype))
    for name, factor in factors.items():
        out[name] = (out[name] * factor).astype(out[name].dtype)
    return out
```

```python
from contextlib import ExitStack

import concourse.bass as bass
from concourse import mybir
import numpy as np

F32 = mybir.dt.float32
F32R = mybir.dt.float32r
BF16 = mybir.dt.bfloat16
I32 = mybir.dt.int32
ALU = mybir.AluOpType
ACT = mybir.ActivationFunctionType
AX = mybir.AxisListType

P = 128
SEQ = 256
NT = SEQ // P
D = 1024
KC = D // P
DFF = 2816
NG = DFF // 256
UW = 2048
RING = 3
AHEAD = RING - 1
EPS = 1e-6
HD = 64
NEG = -1e30

N_Q, N_KV, N_MEM = 12, 3, 4
Q0, K0, V0, QM0 = 0, 768, 960, 1152
W_IN1 = 1408
KM0, VM0 = W_IN1, W_IN1 + 256
W_IN2 = 2290
A_H, A_QR, A_KVR, A_NOPE, A_ROPE = 6, 192, 128, 64, 32
A_DK = A_NOPE + A_ROPE
B0 = A_QR + A_KVR + A_ROPE
B_H, B_G = 6, 2
B_KC, B_VC, B_KS, B_VS, B_KW, B_VW = (B0 + 384 + 128 * j for j in range(6))
B_GATE = B0 + 384 + 768
C0 = B_GATE + 18
C_H, C_D = 4, 32
C_K, C_V = C0 + 256, C0 + 512
N_CMP, CMP_LEN, CMP_STRIDE = 15, 32, 16

UNITS1 = [(QM0, 256), (K0, 256), (Q0 + 512, 256), (Q0, 256), (Q0 + 256, 256), (K0 + 128, 128)]
UNITS2 = [(C0, 256), (C_K, 256), (C_V, 256), (0, 256), (256, 256), (512, 256), (768, 256),
          (1024, 256), (C0 - 256, C0 - 1280)]

FULL, CAUSAL, BAND = "full", "causal", "band"
BLOCKS = {FULL: [(0, 0), (0, 1), (1, 0), (1, 1)], BAND: [(0, 0), (0, 1), (1, 0), (1, 1)],
          CAUSAL: [(0, 0), (1, 0), (1, 1)]}
TURNED_AT = {FULL: [0, 256, 128, 384], BAND: [0, 256, 128, 384], CAUSAL: [0, 128, 256]}
MASKED = {FULL: {}, CAUSAL: {0: "upper", 2: "upper"}, BAND: {1: "upper", 2: "lower"}}
ORDER = [6, 7, 0, 1, 2, 3, 4, 5]

C_ID, C_CM, C_RV, C_RP, C_AX, C_IF, C_UP, C_LO = np.cumsum([0, 128, 30, 2, 32, 128, 28, 128]).tolist()
C_W = C_UP


def constants():
    f = np.float32
    c = np.zeros((P, C_LO + P), f)
    i = np.arange(P)
    c[:, C_ID:C_ID + P] = np.eye(P, dtype=f)
    c[:, C_UP:C_UP + P] = np.where(i[None, :] > i[:, None], f(NEG), f(0))
    c[:, C_LO:C_LO + P] = np.where(i[None, :] < i[:, None], f(NEG), f(0))
    pos = np.arange(SEQ).reshape(NT, P).T
    ends = np.arange(N_CMP) * CMP_STRIDE + CMP_LEN - 1
    c[:, C_CM:C_CM + 30] = np.where(ends <= pos[:, :, None], f(0), f(NEG)).reshape(P, 30)
    c[:, C_RV:C_RV + 2] = pos >= CMP_LEN - 1

    def freq(n, theta):
        return f(theta) ** (-(np.arange(0, n, 2, dtype=f) / f(n)))
    a = pos[:, :, None].astype(f) * freq(16, 500000.0)
    c[:, C_RP:C_RP + 32] = np.stack([np.cos(a), np.sin(a)], 2).reshape(P, 32)
    fa = freq(32, 10000.0)
    a = np.stack([(pos // 64)[:, :, None].astype(f) * fa, (pos % 64)[:, :, None].astype(f) * fa], 2)
    c[:, C_AX:C_AX + 128] = np.stack([np.cos(a), np.sin(a)], 2).reshape(P, 128)
    inv = [f(1) / (f(500000.0) ** (np.arange(0, n, 2, dtype=f) / f(n))) for n in (32, 16, 8)]
    c[:, C_IF:C_IF + 28] = np.concatenate(inv)
    return c


class Signal:

    def __init__(self, name, sem, noted):
        self.name, self.sem, self.noted, self.n = name, sem, noted, 0

    def mark(self, key=None, by=1):
        self.n += by
        self.noted[self.name, key] = self.n
        return by

    def at(self, key):
        return self.noted.get((self.name, key), 1)


class Unit:

    def __init__(self, q, k, rows, value, kind, chunk, half, opens=True, closes=True, factor=None):
        self.q, self.k, self.rows, self.value, self.kind = q, k, rows, value, kind
        self.chunk, self.half, self.opens, self.closes, self.factor = chunk, half, opens, closes, factor
        self.fills = closes and half == 1


class Window:

    def __init__(self, src, col, width, bands):
        self.src, self.col, self.width, self.bands = src, col, width, bands


class Part:

    def __init__(self, windows, units, tasks):
        self.pairs = [windows[i:i + 2] for i in range(0, len(windows), 2)]
        self.units, self.tasks = units, tasks
        self.sequence = [t for step in sorted(tasks) for t in tasks[step]]
        self.filled_by = {}
        for p, pair in enumerate(self.pairs):
            for w in pair:
                for band in w.bands:
                    self.filled_by.setdefault(band[0], []).append(p)

    def bank(self, task):
        return self.sequence.index(task) % 2

    def before(self, task):
        i = self.sequence.index(task)
        return self.sequence[i - 2] if i >= 2 else None

    def pairs_for(self, n, first_use):
        u = self.units[n]
        reused = [p for p in self.filled_by[u.q] if first_use(p) < n]
        need = reused + [p for p in self.filled_by[u.k] if first_use(p) < n]
        return {odd: max([p for p in need if p % 2 == odd], default=None) for odd in (0, 1)}

    def step_of(self, p):
        return [s for s in self.tasks if ("windows", p) in self.tasks[s]][0]


def first_part(kind):
    s = HD ** -0.5
    windows = [Window("proj", QM0 + P * i, P, [(6 + i, 0, P, s)]) for i in range(2)]
    windows += [Window("proj", KM0 + P * i, P, [(22 + 2 * i, 0, HD, 1.0), (23 + 2 * i, HD, P, 1.0)])
                for i in range(2)]
    windows += [Window("proj", K0 - HD, P, [(17, HD, P, 1.0)]),
                Window("proj", K0, P, [(16, 0, HD, 1.0), (19, HD, P, 1.0)]),
                Window("proj", K0 + HD, P, [(18, 0, HD, 1.0), (21, HD, P, 1.0)]),
                Window("proj", K0 + 2 * HD, P, [(20, 0, HD, 1.0)])]
    windows += [Window("proj", Q0 + P * i, P, [(i, 0, P, s)]) for i in range(6)]
    units = []
    for i in range(N_MEM):
        units.append(Unit(6 + i // 2, 22 + i, P, ("proj", VM0 + HD * i), FULL, 6 + i // 2, i % 2))
    for i in range(N_Q):
        units.append(Unit(i // 2, 16 + 2 * (i // 4) + i % 2, P, ("proj", V0 + HD * (i // 4)), kind,
                          i // 2, i % 2, factor=("sink", i) if kind == BAND else None))
    steps = {-1: [0, 1], 0: [2], 1: [4], 2: [3], 3: [5], 4: [6]}
    return Part(windows, units, {k: [("windows", p) for p in v] for k, v in steps.items()})


def second_part():
    s = HD ** -0.5
    windows = [Window("proj", C0 + P * i, P, [(i, 0, P, C_D ** -0.5)]) for i in range(2)]
    windows += [Window("proj", C_K + P * i, P,
                       [(16 + 4 * i + j, C_D * j, C_D * (j + 1), 1.0) for j in range(4)]) for i in range(2)]
    for col, first in ((B_KC, 28), (B_VC, 30)):
        windows += [Window("proj", col, P, [(first, 0, HD, 1.0), (first + 1, HD, P, 1.0)]),
                    Window("proj", col - HD, P, [(first, HD, P, 1.0)]),
                    Window("proj", col + HD, P, [(first + 1, 0, HD, 1.0)])]
    for i in range(A_H):
        windows += [Window("q96", A_DK * i, A_DK, [(2 + i, 0, A_DK, A_DK ** -0.5)]),
                    Window("k96", A_DK * i, A_DK, [(8 + i, 0, A_DK, 1.0)])]
    windows += [Window("proj", col + HD * g, P, [(first + g, 0, HD, 1.0)])
                for col, first in ((B_KS, 24), (B_KW, 26)) for g in range(B_G)]
    q_slots = (14, 15, 0, 1, 2, 3)
    windows += [Window("proj", B0 + HD * i, P, [(q_slots[i], 0, P, s)]) for i in range(B_H)]
    units = []
    for i in range(2 * C_H):
        h = i // 2
        units.append(Unit(i // 4, 16 + i, P, ("proj", C_V + HD * h), CAUSAL, 6 + h // 2, h % 2,
                          i % 2 == 0, i % 2 == 1, ("lambda",) if i % 2 else None))
    for i in range(A_H):
        units.append(Unit(2 + i, 8 + i, A_DK, ("v6", HD * i), CAUSAL, i // 2, i % 2))
    for i in range(B_H):
        g = i // (B_H // B_G)
        for j, (k, v) in enumerate(((24, B_VS), (26, B_VW))):
            units.append(Unit(q_slots[i], k + g, P, ("proj", v + HD * g), CAUSAL, 3 + i // 2, i % 2,
                              False, j == 1, ("gate", i, 1 + j)))
    tasks = {-1: [0, 1], 0: [2, ("pe",)], 1: [3], 2: [4], 3: [5], 4: [6], 5: [7], 6: [8, ("cmp1", 0)],
             7: [9, ("cmp1", 1)], 8: [10, ("back", 6)], 9: [11, ("cmp2", 0)], 10: [12, ("cmp2", 1)],
             11: [13, ("forth", 6)], 12: [14, ("back", 7)], 13: [15], 14: [("scores",)], 16: [("pc", 0), ("forth", 7)]}
    for i in range(1, B_H):
        tasks[16 + 2 * i] = [("pc", i)]
    return Part(windows, units, {k: [("windows", t) if isinstance(t, int) else t for t in v]
                                 for k, v in tasks.items()})


SPARSE0 = 2 * C_H + A_H


def heads(view, n):
    return view.rearrange("p t (h w) -> p t h w", h=n)


def build(nc, a, noted):
    with ExitStack() as ctx:
        room = [16512]

        def sb(name, cols, dt=F32, at=None):
            size = cols * (2 if dt == BF16 else 4)
            if at is None:
                at = room[0]
                room[0] += -(-size // 32) * 32
            return nc.alloc_sbuf_tensor_at(name, [P, cols], dt, offset=at)

        raw = [sb(f"raw{s}", UW) for s in range(RING)]
        w_hi = [sb(f"w_hi{s}", UW, F32R) for s in range(RING)]
        w_lo = [sb(f"w_lo{s}", UW, F32R) for s in range(RING)]
        x_at = sb("x", NT * D)
        h_at = sb("h", NT * D)
        xt_hi, xt_lo = sb("xt_hi", KC * SEQ, F32R), sb("xt_lo", KC * SEQ, F32R)
        xt_end = room[0]
        gain = [sb(f"gain{s}", D) for s in range(2)]
        junk_at = room[0]
        junk = sb("junk", D)
        cst = sb("cst", C_W)
        ident_b, up_b, lo_b = (sb(n, P, BF16) for n in ("ident_b", "up_b", "lo_b"))
        sumsq, rstd = sb("sumsq", 96), sb("rstd", 96)
        half, half_rstd = sb("half", 96), sb("half_rstd", NT)
        gains_t, ones = sb("gains_t", 88), sb("ones", P)
        negmax, rowsum, coef = sb("negmax", 64), sb("rowsum", 64), sb("coef", 64)
        qk_gain = sb("qk_gain", 2 * HD)
        sink = sb("sink", N_Q)
        sinkt, less_sink = sb("sinkt", 2 * N_Q), sb("less_sink", N_Q)
        lam = sb("lam", 16)
        angle = sb("angle", 56 * 2)
        cos2, sin2 = sb("cos2", 56), sb("sin2", 56)
        posi, posf = sb("posi", NT, I32), sb("posf", NT)
        o_base = room[0]
        osum = sb("osum", NT * D)
        phi1 = [sb(f"phi1_{w}", CMP_LEN * HD // 2, at=o_base + 4096 * i) for i, w in enumerate("kv")]
        proj_at = sb("proj", NT * W_IN2)
        f_base = room[0]
        qkt = sb("qkt", 28 * SEQ)
        probs = [sb(f"probs{s}", 512) for s in range(3)]
        probs_t = [sb(f"probs_t{s}", 512) for s in range(2)]
        hid_hi = [sb(f"hid_hi{s}", 512, F32R, at=f_base + 2048 * s) for s in range(2)]
        hid_lo = [sb(f"hid_lo{s}", 512, F32R, at=f_base + 2048 * (2 + s)) for s in range(2)]
        act_g = [sb(f"act_g{s}", 512, at=f_base + 2048 * (4 + s)) for s in range(2)]
        hid = [sb(f"hid{s}", 512, at=f_base + 2048 * (6 + s)) for s in range(2)]
        m_base = room[0]
        mem_hi, mem_lo = sb("mem_hi", KC * SEQ, F32R), sb("mem_lo", KC * SEQ, F32R)
        qk_table = sb("qk_table", 8 * HD)
        qk_table_end = room[0]
        room[0] = m_base
        h_base = 16512 + 4 * (3 * RING * UW + NT * D)
        kcv_t = sb("kcv_t", 4 * SEQ, at=h_base)
        v6 = sb("v6", NT * A_H * HD, at=h_base + 4096)
        q96, k96 = sb("q96", NT * A_H * A_DK), sb("k96", NT * A_H * A_DK)
        uq, ukv = sb("uq", 2 * 576), sb("ukv", 768)
        k_cmp, v_cmp = sb("k_cmp", B_G * N_CMP), sb("v_cmp", B_G * HD)
        pe_t = sb("pe_t", 2 * 16, at=h_base + 7168)
        hid_c = [sb(f"hid_c{i}", 30, at=h_base + 7296 + 128 * i) for i in range(2)]
        lat_t = sb("lat_t", 6 * P, at=f_base + 28 * 1024)
        blk = [sb(f"blk{i}", 480, at=junk_at + 2048 * i) for i in range(2)]
        s_cmp = sb("s_cmp", 180 + 128, at=m_base)
        diff_t, diff_r, pc0 = (sb(n, SEQ, at=xt_end - 1024 * (KC - 3 - i))
                               for i, n in enumerate(("diff_t", "diff_r", "pc_t0")))
        pc_t = [pc0, sb("pc_t1", SEQ, at=xt_end - 1024 * (2 * KC - 5))]
        pe_rows = sb("pe_rows", 2 * P)
        phi2 = sb("phi2", 2 * HD)
        small = sb("small", A_QR + A_KVR + HD)
        lamv = sb("lamv", 4 * C_D)
        gate = sb("gate", 36)
        cmp_max, cmp_coef = sb("cmp_max", 12), sb("cmp_coef", 12)
        assert max(room[0], qk_table_end) <= 229368, room[0]

        bank = [ctx.enter_context(nc.psum_tensor(f"bank{i}", [P, 512], F32)) for i in range(8)]
        G_B, U_B, ACC = bank[0:2], bank[2:4], bank[4:8]
        TURN = bank[0:4]
        S_B, PT_B, O_B, QT_B = bank[0:2], bank[2:4], bank[4:6], bank[6:8]

        x = x_at[:, :].rearrange("p (t n) -> p t n", t=NT)
        h = h_at[:, :].rearrange("p (t n) -> p t n", t=NT)
        osm = osum[:, :].rearrange("p (t n) -> p t n", t=NT)
        proj = proj_at[:, :].rearrange("p (t n) -> p t n", t=NT)
        ident = cst[:, C_ID:C_ID + P]

        gate4 = gate[:, :].rearrange("p (t h k) -> p t h k", t=NT, k=3)
        OUT = ("o", "o2")
        QK_PIECES = {1: (K0, N_KV), 2: (Q0 + 512, 4), 3: (Q0, 4), 4: (Q0 + 256, 4)}

        def xt_chunk(t, c, which):
            return which[:, c * SEQ + t * P:c * SEQ + (t + 1) * P]

        units = []

        def columns(w, first):
            return w[:, bass.ds(first, 256)].rearrange("(c p) n -> p c n", p=P)

        def rows(w, first):
            return w[bass.ds(first, 256), :].rearrange("(m p) n -> p m n", p=P)

        def plan_projection(w, parts):
            for first, _ in parts:
                units.append(columns(w, first))

        WHOLE = [(c, 256) for c in range(0, D, 256)]
        ffns = []

        def plan_ffn(wg, wu, wd, last=False):
            ffns.append((len(units), wg, wu, wd, last))
            units.extend([None] * (3 * NG))

        for l in range(2):
            plan_projection(a["w_mem_kv"][l], ((0, 256), (256, 256)))
            plan_projection(a["w_in"][l], UNITS1)
            plan_projection(a["w_o"][l], WHOLE)
            gu = a["w_gate_up"][l]
            plan_ffn(gu[:, 0:DFF], gu[:, DFF:2 * DFF], a["w_down"][l])
        for l in range(2):
            plan_ffn(a["ffn1_wg_2"][l], a["ffn1_wu_2"][l], a["ffn1_wd_2"][l])
            plan_projection(a["w_in_2"][l], UNITS2)
            plan_projection(a["w_out_2"][l], WHOLE)
            plan_ffn(a["ffn2_wg_2"][l], a["ffn2_wu_2"][l], a["ffn2_wd_2"][l], last=(l == 1))
        TOTAL = len(units)

        BEFORE = [0, 1, 5, 3, 7, 9, 12, 10, 13, 11, 14]
        gain_rows = [a["mem_norm_g"].rearrange("(c p) -> c p", p=P)] + [
            a[n].rearrange("l (c p) -> (l c) p", p=P)
            for n in ("g_mix_pre", "g_ffn_pre", "ffn1_norm_2", "mix_norm_2", "ffn2_norm_2")]
        gains = [a["g_mix_post"][0], a["g_ffn_post"][0], a["g_mix_post"][1], a["g_ffn_post"][1],
                 a["final_norm_2"]]
        GAIN_USED = [("osum", 0), ("fsum", 0), ("osum", 1), ("fsum", 1)]

        def norm_column(j):
            return 64 + 2 * j

        def norm_of(f):
            return 3 + 4 * f if f < 2 else 9 + 3 * (f // 2 - 1) + 2 * (f % 2)

        def sem(name):
            return ctx.enter_context(nc.semaphore(name))

        def sig(name):
            return Signal(name, sem(name), noted)

        raw_landed = [sem(f"raw_landed{s}") for s in range(RING)]
        hi_ready, lo_ready, unit_used = sem("hi_ready"), sem("lo_ready"), sem("unit_used")
        gates_ready, silu_ready, hidden_ready, hidden_hi, hidden_lo, half_used = (
            sem(n) for n in ("gates_ready", "silu_ready", "hidden_ready", "hidden_hi", "hidden_lo",
                             "half_used"))
        consts_landed, rows_landed, tables_landed, x_landed, mem_landed = (
            sem(n) for n in ("consts_landed", "rows_landed", "tables_landed", "x_landed", "mem_landed"))
        gain_landed = [sem(f"gain_landed{s}") for s in range(2)]
        layer_landed, phi_landed = sem("layer_landed"), sem("phi_landed")
        out_stored = sem("out_stored")
        squares, head_squares, rstd_ready = sig("squares"), sig("head_squares"), sig("rstd_ready")
        rows_ready, turned, turned_hi, turned_lo = (
            sig(n) for n in ("rows_ready", "turned", "turned_hi", "turned_lo"))
        proj_out, prep_ready, small_act = sig("proj_out"), sig("prep_ready"), sig("small_act")
        heads_turned, heads_out_a, heads_out_v = (
            sig(n) for n in ("heads_turned", "heads_out_a", "heads_out_v"))
        scores_ready, negmax_ready, probs_ready, probs_scaled, probs_turned, probs_out_a, probs_out_v = (
            sig(n) for n in ("scores_ready", "negmax_ready", "probs_ready", "probs_scaled",
                             "probs_turned", "probs_out_a", "probs_out_v"))
        values_ready, small_mm, dve_order, pool_order, task_out_a, task_out_v, sink_shift = (
            sig(n) for n in ("values_ready", "small_mm", "dve_order", "pool_order", "task_out_a",
                             "task_out_v", "sink_shift"))

        FIRST0, FIRST1, SECOND = first_part(BAND), first_part(FULL), second_part()

        def token_rows(src, t, col, width):
            if src == "proj":
                return proj[:, t, col:col + width]
            which, n = {"q96": (q96, A_H * A_DK), "k96": (k96, A_H * A_DK), "v6": (v6, A_H * HD)}[src]
            return which[:, t * n + col:t * n + col + width]

        def slot(i, first, last, lo=0, hi=SEQ):
            if i >= 28:
                return kcv_t[first:last, (i - 28) * SEQ + lo:(i - 28) * SEQ + hi]
            return qkt[first:last, i * SEQ + lo:i * SEQ + hi]

        def out_by_scalar(second, m):
            return second or m % 2 == 0

        rstd_rows, rstd_diag = proj_at[:, 0:SEQ], junk[:, 0:SEQ]

        def gain_t(j, c):
            i = 8 * BEFORE.index(j) + c
            return gains_t[:, i:i + 1]

        def chunk(which, c):
            return which[:, SEQ * c:SEQ * (c + 1)]

        def gate_done(u0, g):
            return u0 + 1 if isinstance(g, int) and g == 0 else 3 * g + u0

        def scores_at(kind, t):
            ix = [i for i, b in enumerate(BLOCKS[kind]) if b[0] == t]
            return ix[0] * P, len(ix) * P

        block = ctx.enter_context(nc.Block())

        @block.sync
        def _(sp):
            sp.dma_start(cst[:, :], a["constants"][:, 0:C_W]).then_inc(consts_landed, 16)
            at = 0
            for src in gain_rows:
                n = src.shape[0]
                sp.dma_start(proj_at[at:at + n, 512:640], src).then_inc(rows_landed, 16)
                at += n
            sp.dma_start(h, a["mem"][0].rearrange("(t p) n -> p t n", p=P)).then_inc(mem_landed, 16)
            sp.dma_start(proj_at[:, 0:2 * P], a["constants"][:, C_UP:]).then_inc(consts_landed, 16)

            def load(u, src, i=0):
                s = u % RING
                if u >= RING:
                    sp.wait_ge(lo_ready, 6 * i + (u - RING + 1))
                parts = src.shape[1]
                sp.dma_start(raw[s][:, :].rearrange("p (c n) -> p c n", c=parts), src)\
                  .then_inc(raw_landed[s], 16)

            u = 0
            starts = {f[0]: f for f in ffns}
            while u < TOTAL:
                if u == 2:
                    sp.dma_start(x, a["x"][0].rearrange("(t p) n -> p t n", p=P)).then_inc(x_landed, 16)
                if u not in starts:
                    load(u, units[u])
                    u += 1
                    continue
                _, wg, wu, wd, _ = starts[u]
                load(u, columns(wg, 0))
                load(u + 1, columns(wu, 0))
                load(u + 2, columns(wg, 256))
                load(u + 3, columns(wu, 256))
                load(u + 4, rows(wd, 0))
                with sp.Fori(0, 4) as i:
                    for j in range(2):
                        load(u + 5 + 3 * j, columns(wg, 512 * i + 256 * (j + 2)), i)
                        load(u + 6 + 3 * j, columns(wu, 512 * i + 256 * (j + 2)), i)
                        load(u + 7 + 3 * j, rows(wd, 512 * i + 256 * (j + 1)), i)
                load(u + 29, columns(wg, 256 * 10))
                load(u + 30, columns(wu, 256 * 10))
                load(u + 31, rows(wd, 256 * 9))
                load(u + 32, rows(wd, 256 * 10))
                u += 3 * NG
            for t in range(NT):
                sp.wait_ge(rows_ready.sem, rows_ready.at(("final", t)))
                sp.dma_start(a["out"][0, P * t:P * (t + 1), :], h[:, t, :]).then_inc(out_stored, 16)
            sp.wait_ge(out_stored, 16 * NT)

        @block.gpsimd
        def _(pool):
            def zero(view, key):
                pool.memset(view, 0.0).then_inc(pool_order.sem, pool_order.mark(key))

            def load_gain(j):
                if j >= 2:
                    pool.wait_ge(prep_ready.sem, prep_ready.at(GAIN_USED[j - 2]))
                pool.dma_start(gain[j % 2][:, :], gains[j].partition_broadcast(P))\
                    .then_inc(gain_landed[j % 2], 16)

            def power(scales, key, source=squares):
                pool.wait_ge(source.sem, source.at(key))
                for lo, hi, n in scales:
                    pool.tensor_scalar(sumsq[:, lo:hi], sumsq[:, lo:hi], 1.0 / n, EPS, ALU.mult,
                                       ALU.add).then_inc(pool_order.sem, pool_order.mark())
                pool.wait_ge(pool_order.sem, pool_order.n)
                lo, hi = scales[0][0], scales[-1][1]
                pool.tensor_tensor(rstd[:, lo:hi], sumsq[:, lo:hi], half[:, lo:hi], ALU.pow)\
                    .then_inc(rstd_ready.sem, rstd_ready.mark(key))

            pool.memset(half[:, :], -0.5).then_inc(pool_order.sem, pool_order.mark())
            pool.memset(ones[:, :], 1.0).then_inc(pool_order.sem, pool_order.mark("ones"))
            pool.dma_start(qk_gain[:, :], a["qk_norm_g"][0].rearrange("a b -> (a b)").partition_broadcast(P))\
                .then_inc(tables_landed, 16)
            pool.dma_start(sink[:, :], a["attn_sink"][0].partition_broadcast(P)).then_inc(tables_landed, 16)
            pool.dma_start(posi[:, :], a["positions_2"][0].rearrange("(t p) -> p t", p=P),
                           allow_slow_non_contiguous=True)\
                .then_inc(tables_landed, 16)
            load_gain(0)
            load_gain(1)
            zero(qkt[:, 16 * SEQ:28 * SEQ], "zero1")

            def norm(j, source=squares):
                c = norm_column(j)
                power([(c, c + 2, D)], ("norm", j), source)

            norm(0)
            for l in range(2):
                norm(1 + 4 * l)
                if l == 1:
                    for piece in range(4):
                        power([(32 + 8 * piece, 40 + 8 * piece, HD)], ("qk", piece), head_squares)
                norm(2 + 4 * l, head_squares)
                if l:
                    load_gain(3)
                norm(3 + 4 * l)
                norm(4 + 4 * l, head_squares)
                load_gain(2 + 2 * l)
            for l in range(2):
                norm(9 + 3 * l)
                if l:
                    pool.wait_ge(turned_lo.sem, turned_lo.at(("o2", 0, 7)))
                else:
                    pool.wait_ge(prep_ready.sem, prep_ready.at(("rows", ("ffn1", 0), 3)))
                for dst, src in (
                    (uq[:, 0:576], a["mla_w_uq_2"][l, 0:P, :]),
                    (uq[0:HD, 576:1152], a["mla_w_uq_2"][l, P:A_QR, :]),
                    (ukv[:, :], a["mla_w_ukv_2"][l]),
                    (small[:, 0:A_QR], a["mla_q_norm_2"][l].partition_broadcast(P)),
                    (small[:, A_QR:A_QR + A_KVR], a["mla_kv_norm_2"][l].partition_broadcast(P)),
                    (small[:, A_QR + A_KVR:], a["diff_sub_norm_2"][l].partition_broadcast(P)),
                    (lamv[:, 0:32], a["diff_lq1_2"][l].partition_broadcast(P)),
                    (lamv[:, 32:64], a["diff_lk1_2"][l].partition_broadcast(P)),
                    (lamv[:, 64:96], a["diff_lq2_2"][l].partition_broadcast(P)),
                    (lamv[:, 96:128], a["diff_lk2_2"][l].partition_broadcast(P)),
                ):
                    pool.dma_start(dst, src).then_inc(layer_landed, 16)
                for w, which in enumerate("kv"):
                    for dst, src in (
                        (phi1[w][:, :].rearrange("p (o n) -> p o n", n=HD),
                         a[f"nsa_phi_{which}1_2"][l].rearrange("(o p) n -> p o n", p=P)),
                        (phi2[0:HD, HD * w:HD * (w + 1)], a[f"nsa_phi_{which}2_2"][l]),
                        (pe_rows[0:16, P * w:P * (w + 1)],
                         a[f"nsa_pe_{which}_2"][l].rearrange("(o l) d -> o (l d)", l=2)),
                    ):
                        pool.dma_start(dst, src).then_inc(phi_landed, 16)
                if l == 0:
                    for view in (qkt[:, 16 * SEQ:28 * SEQ], k_cmp[:, :], v_cmp[:, :]):
                        zero(view, "zero2")
                norm(10 + 3 * l)
                power([(12, 14, A_QR), (14, 16, A_KVR)], ("latent", l))
                for c in (6, 7):
                    power([(4 * c - 8, 4 * c - 4, HD)], ("sub", l, c), head_squares)
                norm(11 + 3 * l)
            norm(15)

        @block.scalar
        def _(act):
            def split_hi(u, i=0):
                s = u % RING
                act.wait_ge(raw_landed[s], 16 * (u // RING + 1) + 32 * i)
                if u >= RING:
                    act.wait_ge(unit_used, u - RING + 1 + 6 * i)
                act.activation(w_hi[s][:, :], raw[s][:, :], ACT.Copy).then_inc(hi_ready, 1)

            def squares_of(src, j):
                for t in range(NT):
                    c = norm_column(j) + t
                    act.activation(junk[:, :], src[:, t, :], ACT.Square, accum_out=sumsq[:, c:c + 1])\
                       .then_inc(squares.sem, squares.mark(("norm", j)))
                    act.wait_ge(squares.sem, squares.n)

            def turn_hi(name, j, hi=xt_hi, used=None):
                for p in range(4):
                    act.wait_ge(turned.sem, turned.at((name, p)))
                    if used and p == 0:
                        act.wait_ge(unit_used, used)
                    for e in range(2):
                        c = 2 * p + e
                        act.activation(chunk(hi, c), TURN[p][:, SEQ * e:SEQ * (e + 1)], ACT.Copy,
                                       scale=gain_t(j, c))\
                           .then_inc(turned_hi.sem, turned_hi.mark((name, p)))

            def projection(u0, parts, col0, k0, j, after=None):
                n = norm_column(j)
                factor = [rstd[:, n + t:n + t + 1] for t in range(NT)]
                for k, (first, new) in enumerate(parts):
                    if u0 + k + AHEAD < TOTAL:
                        split_hi(u0 + k + AHEAD)
                    act.wait_ge(unit_used, u0 + k + 1)
                    if k == 0:
                        act.wait_ge(rstd_ready.sem, rstd_ready.at(("norm", j)))
                    src = ACC[(k0 + k) % 4][:, :].rearrange("p (t n) -> p t n", t=NT)
                    col = col0 + first + 256 - new
                    if l == 1 and k in QK_PIECES and parts is UNITS1:
                        if k > 2:
                            act.wait_ge(head_squares.sem, head_squares.at(("qk", k - 3)))
                        for t in range(NT):
                            o = 512 * (k % 2) + 256 * t
                            act.activation(osum[:, o:o + 256], src[:, t, :], ACT.Square, scale=factor[t])\
                               .then_inc(small_act.sem, small_act.mark(("qk squares", k)))
                    for t in range(NT):
                        act.activation(proj[:, t, col:col + new], src[:, t, 256 - new:], ACT.Copy,
                                       scale=factor[t])\
                           .then_inc(proj_out.sem, proj_out.mark(("unit", u0 + k)))
                    if after and k in after:
                        after[k]()

            def out_projection(u0, norm=False):
                for k in range(4):
                    split_hi(u0 + k + AHEAD)
                    if norm:
                        act.wait_ge(unit_used, u0 + k + 1)
                        for t in range(NT):
                            c = 16 + 4 * t + k
                            act.activation(junk[:, 0:256], ACC[k][:, 256 * t:256 * (t + 1)], ACT.Square,
                                           accum_out=sumsq[:, c:c + 1])\
                               .then_inc(squares.sem, squares.mark(("piece", l, k)))
                            act.wait_ge(squares.sem, squares.n)

            def ffn(f):
                u0, _, _, _, last = ffns[f]
                base = NG * f

                def group(g, p):
                    act.wait_ge(gates_ready, base + g + 1)
                    act.activation(act_g[p][:, :], hid[p][:, :], ACT.Silu).then_inc(silu_ready, 1)
                    act.wait_ge(hidden_ready, base + g + 1)
                    act.activation(hid_hi[p][:, :], hid[p][:, :], ACT.Copy).then_inc(hidden_hi, 1)

                split_hi(u0 + 2)
                split_hi(u0 + 3)
                group(0, 0)
                split_hi(u0 + 4)
                split_hi(u0 + 5)
                group(1, 1)
                split_hi(u0 + 6)
                with act.Fori(0, 4) as i:
                    for j in range(2):
                        split_hi(u0 + 7 + 3 * j, i)
                        split_hi(u0 + 8 + 3 * j, i)
                        group(2 * i + j + 2, j)
                        split_hi(u0 + 9 + 3 * j, i)
                split_hi(u0 + 31)
                split_hi(u0 + 32)
                group(10, 0)
                if not last:
                    split_hi(u0 + 33)
                    split_hi(u0 + 34)

            def copy_windows(part, l, p):
                act.wait_ge(heads_turned.sem, heads_turned.at((l, part is SECOND, p)))
                for m, w in enumerate(part.pairs[p]):
                    for s, first, end, scale in w.bands:
                        act.activation(slot(s, first, end),
                                       QT_B[part.bank(("windows", p))][first:end, SEQ * m:SEQ * (m + 1)],
                                       ACT.Copy, scale=scale)\
                           .then_inc(heads_out_a.sem, heads_out_a.mark((l, part is SECOND, p)))

            def attend(part, l, hooks={}):
                second = part is SECOND
                N = len(part.units)
                for n in range(N + 3):
                    if n < N:
                        act.wait_ge(negmax_ready.sem, negmax_ready.at((l, second, n)))
                        if n >= 3:
                            act.wait_ge(probs_turned.sem, probs_turned.at((l, second, n - 3)))
                        for t in range(NT):
                            lo, w = scores_at(part.units[n].kind, t)
                            act.activation(probs[n % 3][:, lo:lo + w], S_B[n % 2][:, lo:lo + w], ACT.Exp,
                                           bias=negmax[:, 2 * n + t:2 * n + t + 1],
                                           accum_out=rowsum[:, 2 * n + t:2 * n + t + 1])\
                               .then_inc(probs_ready.sem, probs_ready.mark((l, second, n)))
                        if part is FIRST0 and part.units[n].factor:
                            i = part.units[n].factor[1]
                            act.wait_ge(sink_shift.sem, sink_shift.at(n))
                            act.activation(sinkt[:, 2 * i:2 * i + 2], sinkt[:, 2 * i:2 * i + 2], ACT.Exp)\
                               .then_inc(probs_ready.sem, probs_ready.mark((l, second, n)))
                    if 0 <= n - 2 < N and out_by_scalar(second, n - 2):
                        m = n - 2
                        act.wait_ge(probs_turned.sem, probs_turned.at((l, second, m)))
                        if m >= 2:
                            act.wait_ge(values_ready.sem, values_ready.at((l, second, m - 2)))
                        w = P * len(BLOCKS[part.units[m].kind])
                        act.activation(probs_t[m % 2][:, 0:w], PT_B[m % 2][:, 0:w], ACT.Copy)\
                           .then_inc(probs_out_a.sem, probs_out_a.mark((l, second, m)))
                    for task in part.tasks.get(n, []):
                        if task[0] == "windows" and task[1] % 2 == 0:
                            copy_windows(part, l, task[1])
                    for hook in hooks.get(n, []):
                        hook()
                    if n >= 3 and part.units[n - 3].fills:
                        c = part.units[n - 3].chunk
                        act.wait_ge(values_ready.sem, values_ready.at((l, second, n - 3)))
                        o = O_B[ORDER.index(c) % 2]
                        if second and c >= 6:
                            act.activation(diff_t[:, :], o[:, 0:SEQ], ACT.Copy)\
                               .then_inc(task_out_a.sem, task_out_a.mark((l, "diff", c)))
                        else:
                            act.activation(xt_hi[:, SEQ * c:SEQ * (c + 1)], o[:, 0:SEQ], ACT.Copy)\
                               .then_inc(turned_hi.sem, turned_hi.mark((OUT[second], l, c)))

            split_hi(0)
            split_hi(1)
            act.wait_ge(prep_ready.sem, prep_ready.at("gains_t"))
            turn_hi("mem", 0, mem_hi)
            squares_of(h, 0)
            u = 0
            for l in range(2):
                def turn_x():
                    turn_hi(("mix", l), 1 + 4 * l)
                    squares_of(x, 1 + 4 * l)
                projection(u, ((0, 256), (256, 256)), W_IN1, 2, 0, {0: turn_x})
                part = (FIRST0, FIRST1)[l]
                act.wait_ge(pool_order.sem, pool_order.at("zero1"))
                projection(u + 2, UNITS1, 0, 4, 1 + 4 * l, {4: lambda: copy_windows(part, l, 0)})
                u += 8
                attend(part, l)
                out_projection(u, True)
                u += 4
                turn_hi(("ffn", l), 3 + 4 * l)
                squares_of(x, 3 + 4 * l)
                ffn(l)
                u += 3 * NG
                n = norm_column(3 + 4 * l)
                for b in range(2):
                    if b:
                        act.wait_ge(unit_used, u)
                    else:
                        act.wait_ge(half_used, l + 1)
                    for t in range(NT):
                        c = 16 + 2 * t + b
                        act.activation(junk[:, 256:768], ACC[2 * t + b][:, :], ACT.Square,
                                       scale=rstd[:, n + t:n + t + 1], accum_out=sumsq[:, c:c + 1])\
                           .then_inc(squares.sem, squares.mark(("half", l, b)))
                        act.wait_ge(squares.sem, squares.n)
            act.wait_ge(prep_ready.sem, prep_ready.at("angles"))
            act.activation(sin2[:, :], angle[:, 0:56], ACT.Sin).then_inc(small_act.sem, small_act.mark())
            act.activation(cos2[:, :], angle[:, 56:112], ACT.Sin)\
               .then_inc(small_act.sem, small_act.mark("angles"))
            for l in range(2):
                turn_hi(("ffn1", l), 9 + 3 * l)
                squares_of(x, 9 + 3 * l)
                ffn(2 + 2 * l)
                u += 3 * NG
                turn_hi(("mix2", l), 10 + 3 * l)
                squares_of(x, 10 + 3 * l)

                def latent_squares():
                    act.wait_ge(proj_out.sem, proj_out.n)
                    for t in range(NT):
                        for o, (lo, hi) in ((12, (0, A_QR)), (14, (A_QR, A_QR + A_KVR))):
                            act.activation(junk[:, 512:512 + hi - lo], proj[:, t, lo:hi], ACT.Square,
                                           accum_out=sumsq[:, o + t:o + t + 1])\
                               .then_inc(squares.sem, squares.mark(("latent", l)))
                            act.wait_ge(squares.sem, squares.n)

                def lambdas():
                    act.wait_ge(prep_ready.sem, prep_ready.at(("lam", l)))
                    act.activation(lam[:, 2:4], lam[:, 0:2], ACT.Exp)\
                       .then_inc(small_act.sem, small_act.mark(("lam", l)))

                def latent_queries():
                    copy_windows(SECOND, l, 0)
                    for t in range(NT):
                        for b in range(2):
                            act.wait_ge(small_mm.sem, small_mm.at(("uq", l, t, b)))
                            act.activation(q96[:, t * 576 + 288 * b:t * 576 + 288 * (b + 1)],
                                           bank[2 * t + b][:, 0:288], ACT.Copy)\
                               .then_inc(small_act.sem, small_act.mark(("uq", l)))

                def gates():
                    act.wait_ge(proj_out.sem, proj_out.n)
                    act.activation(gate[:, :].rearrange("p (t n) -> p t n", t=NT),
                                   proj[:, :, B_GATE:B_GATE + 18], ACT.Exp, scale=-1.0)\
                       .then_inc(small_act.sem, small_act.mark(("gate", l)))

                def latent_keys():
                    k6 = k96[:, 0:576].rearrange("p (h w) -> p h w", h=A_H)
                    v3 = v6[:, 0:384].rearrange("p (h w) -> p h w", h=A_H)
                    for b in range(2):
                        act.wait_ge(small_mm.sem, small_mm.at(("ukv", l, 0, b)))
                        kv = bank[b][:, 0:384].rearrange("p (h w) -> p h w", h=3)
                        act.activation(k6[:, 3 * b:3 * b + 3, 0:HD], kv[:, :, 0:HD], ACT.Copy)\
                           .then_inc(small_act.sem, small_act.mark())
                        act.activation(v3[:, 3 * b:3 * b + 3, :], kv[:, :, HD:2 * HD], ACT.Copy)\
                           .then_inc(small_act.sem, small_act.mark(("ukv", l)))

                def hidden_silu():
                    act.wait_ge(small_mm.sem, small_mm.at(("cmp1", l, 1)))
                    for w in range(2):
                        act.activation(hid_c[w][0:HD, :],
                                       QT_B[SECOND.bank(("cmp1", w))][0:HD, 32 * w:32 * w + 30], ACT.Silu)                           .then_inc(small_act.sem, small_act.mark(("cmp", l)))

                def back_out(c):
                    act.wait_ge(small_mm.sem, small_mm.at(("back", l, c)))
                    src = QT_B[SECOND.bank(("back", c))][:, 0:SEQ]
                    act.activation(junk[:, 512:768], src, ACT.Square)\
                       .then_inc(task_out_a.sem, task_out_a.mark())
                    act.activation(diff_r[:, :], src, ACT.Copy)\
                       .then_inc(task_out_a.sem, task_out_a.mark((l, "back", c)))

                def forth_out(c):
                    act.wait_ge(small_mm.sem, small_mm.at(("forth", l, c)))
                    act.activation(xt_hi[:, SEQ * c:SEQ * (c + 1)],
                                   QT_B[SECOND.bank(("forth", c))][:, 0:SEQ], ACT.Copy)\
                       .then_inc(turned_hi.sem, turned_hi.mark(("o2", l, c)))

                def compressed_exp():
                    act.wait_ge(prep_ready.sem, prep_ready.at(("s_cmp", l)))
                    act.activation(s_cmp[:, 0:180], s_cmp[:, 0:180], ACT.Exp)\
                       .then_inc(small_act.sem, small_act.mark(("s_cmp", l)))

                if l == 0:
                    act.wait_ge(pool_order.sem, pool_order.at("zero2"))
                projection(u, UNITS2, 0, 1, 10 + 3 * l, {2: lambdas, 4: latent_squares, 7: latent_queries, 8: gates})
                u += 9
                latent_keys()
                attend(SECOND, l, {7: [hidden_silu], 8: [lambda: back_out(6)], 11: [lambda: forth_out(6)],
                                   12: [lambda: back_out(7)], 14: [compressed_exp],
                                   16: [lambda: forth_out(7)]})
                out_projection(u)
                u += 4
                turn_hi(("ffn2", l), 11 + 3 * l, used=u)
                squares_of(x, 11 + 3 * l)
                ffn(3 + 2 * l)
                u += 3 * NG
            act.wait_ge(prep_ready.sem, prep_ready.at(("rows", "final", 3)))
            squares_of(x, 15)

        @block.vector
        def _(dve):
            def link(ins, signal=dve_order, key=None):
                ins.then_inc(signal.sem, signal.mark(key))
                dve.wait_ge(signal.sem, signal.n)

            def split_lo(u, i=0):
                s = u % RING
                dve.wait_ge(hi_ready, u + 1 + 6 * i)
                dve.tensor_tensor(w_lo[s][:, :], raw[s][:, :], w_hi[s][:, :].bitcast(F32), ALU.subtract)\
                   .then_inc(lo_ready, 1)

            def turn_lo(name, j, hi=xt_hi, lo=xt_lo):
                for p in range(4):
                    dve.wait_ge(turned_hi.sem, turned_hi.at((name, p)))
                    for e in range(2):
                        c = 2 * p + e
                        dve.scalar_tensor_tensor(chunk(lo, c), TURN[p][:, SEQ * e:SEQ * (e + 1)],
                                                 gain_t(j, c), chunk(hi, c).bitcast(F32), ALU.mult,
                                                 ALU.subtract)\
                           .then_inc(turned_lo.sem, turned_lo.mark((name, p)))

            def projection(u0, n, prepare=None):
                for k in range(n):
                    if u0 + k + AHEAD < TOTAL:
                        split_lo(u0 + k + AHEAD)
                    if prepare and k:
                        dve.wait_ge(proj_out.sem, proj_out.at(("unit", u0 + k - 1)))
                        prepare(k - 1)
                if prepare:
                    dve.wait_ge(proj_out.sem, proj_out.at(("unit", u0 + n - 1)))
                    prepare(n - 1)

            def sum_squares(parts, j):
                n = norm_column(j)
                link(dve.tensor_reduce(sumsq[:, n:n + 2],
                                       sumsq[:, 16:16 + 2 * parts].rearrange("p (t k) -> p t k", t=NT), AX.X,
                                       ALU.add), head_squares, ("norm", j))

            def add_norm(j, following):
                dve.wait_ge(rstd_ready.sem, rstd_ready.at(("norm", j)))
                n = norm_column(j)
                for p in range(4):
                    for t in range(NT):
                        xs = x[:, t, 256 * p:256 * (p + 1)]
                        dve.scalar_tensor_tensor(xs, osm[:, t, 256 * p:256 * (p + 1)],
                                                 rstd[:, n + t:n + t + 1], xs, ALU.mult, ALU.add)\
                           .then_inc(prep_ready.sem, prep_ready.mark(("rows", following, p)))

            def ffn(f):
                u0, _, _, _, last = ffns[f]
                base = NG * f

                def gates(g, p):
                    dve.wait_ge(unit_used, gate_done(u0, g))
                    dve.tensor_tensor(hid[p][:, :].rearrange("p (m s) -> p m s", m=2),
                                      G_B[p][:, :].rearrange("p (m s) -> p m s", m=2),
                                      rstd_rows.unsqueeze(1).to_broadcast([P, 2, SEQ]), ALU.mult)\
                       .then_inc(gates_ready, 1)

                def group(g, p):
                    dve.wait_ge(silu_ready, base + g + 1)
                    dve.wait_ge(unit_used, gate_done(u0, g) + 1)
                    dve.tensor_tensor(hid[p][:, :], act_g[p][:, :], U_B[p][:, :], ALU.mult)\
                       .then_inc(hidden_ready, 1)
                    dve.wait_ge(hidden_hi, base + g + 1)
                    dve.tensor_tensor(hid_lo[p][:, :], hid[p][:, :], hid_hi[p][:, :].bitcast(F32),
                                      ALU.subtract).then_inc(hidden_lo, 1)

                n = norm_column(norm_of(f))
                dve.wait_ge(rstd_ready.sem, rstd_ready.at(("norm", norm_of(f))))
                for t in range(NT):
                    link(dve.tensor_scalar(rstd_diag[:, P * t:P * (t + 1)], ident, rstd[:, n + t:n + t + 1],
                                           None, ALU.mult), prep_ready, ("diagonal", f))
                link(dve.tensor_scalar(half_rstd[:, :], rstd[:, n:n + 2], 0.5, None, ALU.mult))
                split_lo(u0 + 2)
                split_lo(u0 + 3)
                dve.wait_ge(small_mm.sem, small_mm.at(("rstd rows", f)))
                link(dve.tensor_copy(rstd_rows, ACC[0][:, 0:SEQ]), prep_ready, ("rstd rows", f))
                gates(0, 0)
                group(0, 0)
                split_lo(u0 + 4)
                gates(1, 1)
                split_lo(u0 + 5)
                group(1, 1)
                split_lo(u0 + 6)
                with dve.Fori(0, 4) as i:
                    for j in range(2):
                        split_lo(u0 + 7 + 3 * j, i)
                        gates(2 * i + j + 2, j)
                        split_lo(u0 + 8 + 3 * j, i)
                        group(2 * i + j + 2, j)
                        split_lo(u0 + 9 + 3 * j, i)
                split_lo(u0 + 31)
                gates(10, 0)
                split_lo(u0 + 32)
                group(10, 0)
                if not last:
                    split_lo(u0 + 33)
                    split_lo(u0 + 34)

            def copy_windows(part, l, p):
                dve.wait_ge(heads_turned.sem, heads_turned.at((l, part is SECOND, p)))
                for m, w in enumerate(part.pairs[p]):
                    for s, first, end, scale in w.bands:
                        dve.tensor_scalar(slot(s, first, end),
                                          QT_B[part.bank(("windows", p))][first:end, SEQ * m:SEQ * (m + 1)],
                                          scale, None, ALU.mult)\
                           .then_inc(heads_out_v.sem, heads_out_v.mark((l, part is SECOND, p)))

            def attend(part, l, hooks={}):
                second = part is SECOND
                N = len(part.units)

                def maximum(n):
                    unit = part.units[n]
                    dve.wait_ge(scores_ready.sem, scores_ready.at((l, second, n)))
                    sink_unit = part is FIRST0 and unit.factor
                    if unit.kind == CAUSAL:
                        for t in range(NT):
                            lo, w = scores_at(unit.kind, t)
                            dve.tensor_reduce(negmax[:, 2 * n + t:2 * n + t + 1], S_B[n % 2][:, lo:lo + w],
                                              AX.X, ALU.max, negate=True)\
                               .then_inc(negmax_ready.sem, negmax_ready.mark())
                    else:
                        dve.tensor_reduce(negmax[:, 2 * n:2 * n + 2],
                                          S_B[n % 2][:, :].rearrange("p (t s) -> p t s", t=NT),
                                          AX.X, ALU.max, negate=True)\
                           .then_inc(negmax_ready.sem, negmax_ready.mark())
                    if sink_unit:
                        i = unit.factor[1]
                        dve.wait_ge(negmax_ready.sem, negmax_ready.n)
                        dve.tensor_scalar(negmax[:, 2 * n:2 * n + 2], negmax[:, 2 * n:2 * n + 2],
                                          less_sink[:, i:i + 1], None, ALU.min)\
                           .then_inc(negmax_ready.sem, negmax_ready.mark())
                        dve.wait_ge(negmax_ready.sem, negmax_ready.n)
                        dve.tensor_scalar(sinkt[:, 2 * i:2 * i + 2], negmax[:, 2 * n:2 * n + 2],
                                          sink[:, i:i + 1], None, ALU.add)\
                           .then_inc(sink_shift.sem, sink_shift.mark(n))
                    negmax_ready.mark((l, second, n), 0)

                def scale(n):
                    unit = part.units[n]
                    c = slice(2 * n, 2 * n + 2)
                    dve.wait_ge(probs_ready.sem, probs_ready.at((l, second, n)))
                    if part is FIRST0 and unit.factor:
                        i = unit.factor[1]
                        link(dve.tensor_tensor(rowsum[:, c], rowsum[:, c], sinkt[:, 2 * i:2 * i + 2], ALU.add))
                    link(dve.reciprocal(coef[:, c], rowsum[:, c]))
                    if unit.factor and unit.factor[0] == "lambda":
                        link(dve.tensor_scalar(coef[:, c], coef[:, c], lam[:, 4:5], None, ALU.mult))
                    if unit.factor and unit.factor[0] == "gate":
                        _, i, k = unit.factor
                        link(dve.tensor_tensor(coef[:, c], coef[:, c], gate4[:, :, i, k], ALU.mult))
                    for t in range(NT):
                        lo, w = scores_at(unit.kind, t)
                        dve.tensor_scalar(probs[n % 3][:, lo:lo + w], probs[n % 3][:, lo:lo + w],
                                          coef[:, 2 * n + t:2 * n + t + 1], None, ALU.mult)\
                           .then_inc(probs_scaled.sem, probs_scaled.mark((l, second, n)))

                for n in range(N + 3):
                    if n < N:
                        maximum(n)
                    if 1 <= n <= N:
                        scale(n - 1)
                    if 0 <= n - 2 < N and not out_by_scalar(second, n - 2):
                        m = n - 2
                        dve.wait_ge(probs_turned.sem, probs_turned.at((l, second, m)))
                        if m >= 2:
                            dve.wait_ge(values_ready.sem, values_ready.at((l, second, m - 2)))
                        w = P * len(BLOCKS[part.units[m].kind])
                        dve.tensor_copy(probs_t[1][:, 0:w], PT_B[1][:, 0:w])\
                           .then_inc(probs_out_v.sem, probs_out_v.mark((l, second, m)))
                    for task in part.tasks.get(n, []):
                        if task[0] == "windows" and task[1] % 2:
                            copy_windows(part, l, task[1])
                    for hook in hooks.get(n, []):
                        hook()
                    if n >= 3 and part.units[n - 3].fills:
                        c = part.units[n - 3].chunk
                        if not (second and c >= 6):
                            chunk_lo((OUT[second], l, c), c, O_B[ORDER.index(c) % 2])

            def chunk_lo(key, c, src):
                dve.wait_ge(turned_hi.sem, turned_hi.at(key))
                cols = slice(SEQ * c, SEQ * (c + 1))
                dve.tensor_tensor(xt_lo[:, cols], src[:, 0:SEQ], xt_hi[:, cols].bitcast(F32), ALU.subtract)\
                   .then_inc(turned_lo.sem, turned_lo.mark(key))

            def rotate(x1, x2, cos, sin, shape, signal=dve_order, key=None):
                n = 1
                for s in shape[1:]:
                    n *= s
                names = " ".join("abcd"[:len(shape) - 1])
                sizes = dict(zip("abcd", shape[1:]))
                t1 = junk[:, 0:n].rearrange(f"p ({names}) -> p {names}", **sizes)
                t2 = junk[:, 256:256 + n].rearrange(f"p ({names}) -> p {names}", **sizes)
                link(dve.tensor_tensor(t1, x1, sin, ALU.mult))
                link(dve.tensor_tensor(t2, x2, sin, ALU.mult))
                link(dve.tensor_tensor(x1, x1, cos, ALU.mult))
                link(dve.tensor_tensor(x1, x1, t2, ALU.subtract))
                link(dve.tensor_tensor(x2, x2, cos, ALU.mult))
                link(dve.tensor_tensor(x2, x2, t1, ALU.add), signal, key)

            dve.wait_ge(small_mm.sem, small_mm.at("gains_t"))
            link(dve.tensor_copy(gains_t[:, :], ACC[3][:, 0:88]), prep_ready, "gains_t")
            dve.wait_ge(consts_landed, 32)
            link(dve.tensor_copy(ident_b[:, :], ident))
            link(dve.tensor_copy(up_b[:, :], proj_at[:, 0:P]))
            link(dve.tensor_copy(lo_b[:, :], proj_at[:, P:2 * P]), prep_ready, "consts")

            def tables():
                dve.wait_ge(tables_landed, 48)
                link(dve.tensor_scalar(less_sink[:, :], sink[:, :], -1.0, None, ALU.mult))
                link(dve.tensor_copy(posf[:, :], posi[:, :]))
                ang, turns, wrk = angle[:, 0:56], angle[:, 56:112], junk[:, 0:56]
                link(dve.tensor_tensor(ang.rearrange("p (t f) -> p t f", t=NT),
                                       cst[:, C_IF:C_IF + 28].unsqueeze(1).to_broadcast([P, NT, 28]),
                                       posf[:, :].unsqueeze(2).to_broadcast([P, NT, 28]), ALU.mult))
                link(dve.tensor_scalar(turns, ang, float(1 / (2 * np.pi)), 12582912.0, ALU.mult, ALU.add))
                link(dve.tensor_scalar(turns, turns, 12582912.0, None, ALU.subtract))
                two_pi = 2 * np.pi
                c1 = 6.28125
                c2 = float(np.float32(np.round((two_pi - c1) * 2 ** 21) / 2 ** 21))
                c3 = float(np.float32(two_pi - c1 - c2))
                for c in (c1, c2, c3):
                    link(dve.scalar_tensor_tensor(ang, turns, -c, ang, ALU.mult, ALU.add))
                link(dve.tensor_scalar(ang, ang, 3.1415925, -3.1415925, ALU.min, ALU.max))
                link(dve.scalar_tensor_tensor(wrk, ang, -1.0, ang, ALU.mult, ALU.max))
                link(dve.tensor_scalar(turns, wrk, -1.0, float(np.pi / 2), ALU.mult, ALU.add),
                     prep_ready, "angles")
                tab = qk_table[:, :].rearrange("p (w t j s f) -> p w t j s f", w=2, t=NT, j=4, s=2)
                axial = cst[:, C_AX:C_AX + 128].rearrange("p (t k s f) -> p t k s f", t=NT, k=2, s=2)
                for w in range(2):
                    g = qk_gain[:, HD * w:HD * (w + 1)].rearrange("p (s x f) -> p s x f", s=2, x=2)
                    for t in range(NT):
                        for j in range(4):
                            link(dve.tensor_tensor(tab[:, w, t, j], axial[:, t, j % 2], g[:, :, j // 2], ALU.mult))

            split_lo(0)
            split_lo(1)
            turn_lo("mem", 0, mem_hi, mem_lo)
            u = 0
            for l in range(2):
                split_lo(u + 2)
                turn_lo(("mix", l), 1 + 4 * l)
                split_lo(u + 3)

                def prepare0(k):
                    if k == 0:
                        tables()
                    if k not in QK_PIECES:
                        return
                    col, n = QK_PIECES[k]
                    v = heads(proj[:, :, col:col + HD * n], n)

                    def table(j):
                        w = cst[:, C_RP:C_RP + 32].rearrange("p (t k f) -> p t k f", t=NT, k=2)[:, :, j, :]
                        return w.unsqueeze(2).to_broadcast([P, NT, n, 8])
                    rotate(v[:, :, :, 0:8], v[:, :, :, 8:16], table(0), table(1), [P, NT, n, 8],
                           prep_ready, ("piece", l, k))

                def prepare1(k):
                    if k in (1, 2, 3, 4):
                        sum_heads(k)
                    if k in (2, 3, 4):
                        norm_heads(k - 1)

                def sum_heads(k):
                    first = 24 + 8 * k
                    dve.wait_ge(small_act.sem, small_act.at(("qk squares", k)))
                    link(dve.tensor_reduce(sumsq[:, first:first + 8],
                                           osum[:, 512 * (k % 2):512 * (k % 2 + 1)]
                                           .rearrange("p (h d) -> p h d", d=HD), AX.X, ALU.add),
                         head_squares, ("qk", k - 1))

                def norm_heads(k):
                    col, n = QK_PIECES[k]
                    first = 24 + 8 * k
                    w = 0 if n == 4 else 1
                    m = 32 * n
                    tab = qk_table[:, :].rearrange("p (w t j s f) -> p w t j s f", w=2, t=NT, j=4, s=2)

                    def steps(t):
                        qk = proj[:, t, col:col + HD * n].rearrange("p (h d) -> p h d", d=HD)
                        factor = rstd[:, first + 4 * t:first + 4 * t + n].unsqueeze(2)
                        q4 = proj[:, t, col:col + HD * n].rearrange("p (h s f) -> p h s f", h=n, s=2)
                        x1, x2 = q4[:, :, :, 0:16], q4[:, :, :, 16:32]
                        c1, s1, c2, s2 = (tab[:, w, t, j].unsqueeze(1).to_broadcast([P, n, 2, 16])
                                          for j in range(4))
                        t1, t2 = (junk[:, o:o + m].rearrange("p (h s f) -> p h s f", h=n, s=2)
                                  for o in (256 * t, 256 * t + 128))
                        return [(qk, qk, factor.to_broadcast([P, n, HD]), ALU.mult),
                                (t1, x1, s1, ALU.mult), (t2, x2, s2, ALU.mult), (x1, x1, c1, ALU.mult),
                                (x1, x1, t2, ALU.subtract), (x2, x2, c2, ALU.mult), (x2, x2, t1, ALU.add)]
                    dve.wait_ge(rstd_ready.sem, rstd_ready.at(("qk", k - 1)))
                    pairs = list(zip(steps(0), steps(1)))
                    for i, pair in enumerate(pairs):
                        for out, in0, in1, op in pair:
                            if i:
                                dve.wait_ge(dve_order.sem, dve_order.n - 1)
                            ins = dve.tensor_tensor(out, in0, in1, op)
                            if i < len(pairs) - 1:
                                ins.then_inc(dve_order.sem, dve_order.mark())
                            else:
                                dve.wait_ge(dve_order.sem, dve_order.n)
                                ins.then_inc(prep_ready.sem, prep_ready.mark(("piece", l, k)))

                part = (FIRST0, FIRST1)[l]
                projection(u + 2, 6, (prepare0, prepare1)[l])
                u += 8
                copy_windows(part, l, 1)
                attend(part, l, {0: [lambda: norm_heads(4)]} if l else {})
                dve.wait_ge(gain_landed[0], 16 * (l + 1))
                for k in range(4):
                    split_lo(u + k + AHEAD)
                    dve.wait_ge(squares.sem, squares.at(("piece", l, k)))
                    if k == 3:
                        sum_squares(4, 2 + 4 * l)
                    link(dve.tensor_tensor(osm[:, :, 256 * k:256 * (k + 1)],
                                           ACC[k][:, :].rearrange("p (t n) -> p t n", t=NT),
                                           gain[0][:, 256 * k:256 * (k + 1)].unsqueeze(1)
                                           .to_broadcast([P, NT, 256]), ALU.mult), prep_ready, ("osum", l))
                u += 4
                add_norm(2 + 4 * l, ("ffn", l))
                turn_lo(("ffn", l), 3 + 4 * l)
                ffn(l)
                u += 3 * NG
                n = norm_column(3 + 4 * l)
                dve.wait_ge(gain_landed[1], 16 * (l + 1))
                for b in range(2):
                    dve.wait_ge(squares.sem, squares.at(("half", l, b)))
                    if b:
                        sum_squares(2, 4 + 4 * l)
                    for t in range(NT):
                        cols = slice(512 * b, 512 * (b + 1))
                        link(dve.scalar_tensor_tensor(osm[:, t, cols], ACC[2 * t + b][:, :],
                                                      rstd[:, n + t:n + t + 1], gain[1][:, cols], ALU.mult,
                                                      ALU.mult), prep_ready, ("fsum", l))
                add_norm(4 + 4 * l, ("mix", 1) if l == 0 else ("ffn1", 0))

            def add_ffn(f, following):
                for b in range(2):
                    if b:
                        dve.wait_ge(unit_used, u)
                    else:
                        dve.wait_ge(half_used, f + 1)
                    for t in range(NT):
                        xs = x[:, t, 512 * b:512 * (b + 1)]
                        dve.scalar_tensor_tensor(xs, ACC[2 * t + b][:, :], half_rstd[:, t:t + 1], xs,
                                                 ALU.mult, ALU.add)\
                           .then_inc(prep_ready.sem, prep_ready.mark(("rows", following, 2 * b)))
                    prep_ready.mark(("rows", following, 2 * b + 1), 0)

            dve.wait_ge(small_act.sem, small_act.at("angles"))
            for l in range(2):
                lam_init = 0.8 - 0.6 * float(np.exp(-0.3 * l))
                turn_lo(("ffn1", l), 9 + 3 * l)
                ffn(2 + 2 * l)
                u += 3 * NG
                add_ffn(2 + 2 * l, ("mix2", l))
                turn_lo(("mix2", l), 10 + 3 * l)

                def table(which, f0, nf, shape, n):
                    v = which[:, :].rearrange("p (t f) -> p t f", t=NT)[:, :, f0:f0 + nf]
                    return v if n is None else v.unsqueeze(2).to_broadcast(shape)

                def rope(view, n, w, f0, nf, key=None):
                    v = heads(view, n)
                    shape = [P, NT, n, nf]
                    rotate(v[:, :, :, 0:nf], v[:, :, :, nf:2 * nf], table(cos2, f0, nf, shape, n),
                           table(sin2, f0, nf, shape, n), shape, prep_ready, key)

                def latents():
                    dve.wait_ge(rstd_ready.sem, rstd_ready.at(("latent", l)))
                    for t in range(NT):
                        for o, (lo, hi) in ((12, (0, A_QR)), (14, (A_QR, A_QR + A_KVR))):
                            link(dve.scalar_tensor_tensor(proj[:, t, lo:hi], proj[:, t, lo:hi],
                                                          rstd[:, o + t:o + t + 1], small[:, lo:hi],
                                                          ALU.mult, ALU.mult), prep_ready, ("latent", l))
                    rope(proj[:, :, A_QR + A_KVR:B0], 1, A_ROPE, 0, 16)

                def latents_out():
                    dve.wait_ge(small_mm.sem, small_mm.at(("latent", l)))
                    link(dve.tensor_copy(lat_t[:, 0:256], bank[2][:, 0:256]))
                    link(dve.tensor_copy(lat_t[0:HD, 256:512], bank[2][0:HD, 256:512]))
                    link(dve.tensor_copy(lat_t[:, 512:768], bank[3][:, 0:256]), prep_ready, ("lat_t", l))

                k6 = k96[:, :].rearrange("p (t h w) -> p t h w", t=NT, h=A_H)

                def latent_keys():
                    for t in range(1, NT):
                        for b in range(2):
                            dve.wait_ge(small_mm.sem, small_mm.at(("ukv", l, t, b)))
                            kv = bank[2 * t + b][:, 0:384].rearrange("p (h w) -> p h w", h=3)
                            dve.tensor_copy(k6[:, t, 3 * b:3 * b + 3, 0:HD], kv[:, :, 0:HD])\
                               .then_inc(prep_ready.sem, prep_ready.mark())
                            dve.tensor_copy(
                                v6[:, t * 384 + 192 * b:t * 384 + 192 * (b + 1)]
                                .rearrange("p (h w) -> p h w", h=3), kv[:, :, HD:2 * HD])\
                               .then_inc(prep_ready.sem, prep_ready.mark(("ukv", l, t, b)))

                def latent_rope():
                    dve.wait_ge(small_act.sem, small_act.at(("uq", l)))
                    q6 = q96[:, :].rearrange("p (t h w) -> p t h w", t=NT, h=A_H)
                    shape = [P, NT, A_H, 16]
                    rotate(q6[:, :, :, HD:HD + 16], q6[:, :, :, HD + 16:A_DK], table(cos2, 0, 16, shape, A_H),
                           table(sin2, 0, 16, shape, A_H), shape, prep_ready, ("latent heads", l))

                def prepare(k):
                    if k == 0:
                        rope(proj[:, :, C0:C0 + 256], 8, C_D, 24, 4)
                        dve.wait_ge(layer_landed, 160 * (l + 1))
                        link(dve.tensor_tensor_reduce(junk[:, 0:C_D], lamv[:, 0:32], lamv[:, 32:64], 1.0, 0.0,
                                                      ALU.mult, ALU.add, lam[:, 0:1]))
                        link(dve.tensor_tensor_reduce(junk[:, 0:C_D], lamv[:, 64:96], lamv[:, 96:128], 1.0,
                                                      0.0, ALU.mult, ALU.add, lam[:, 1:2]),
                             prep_ready, ("lam", l))
                        link(dve.tensor_scalar(small[:, A_QR + A_KVR:], small[:, A_QR + A_KVR:],
                                               1.0 - lam_init, None, ALU.mult))
                    if k == 1:
                        rope(proj[:, :, C_K:C_K + 256], 8, C_D, 24, 4, ("heads", l, 0))
                    if k == 3:
                        dve.wait_ge(small_act.sem, small_act.at(("lam", l)))
                        link(dve.tensor_tensor(lam[:, 4:5], lam[:, 3:4], lam[:, 2:3], ALU.subtract))
                        link(dve.tensor_scalar(lam[:, 4:5], lam[:, 4:5], -lam_init, None, ALU.add))
                    if k == 5:
                        latents()
                        rope(proj[:, :, B0:B0 + 384], 6, HD, 16, 8)
                        for t in range(NT):
                            link(dve.tensor_copy(k6[:, t, :, HD:A_DK],
                                                 proj[:, t, A_QR + A_KVR:B0].unsqueeze(1)
                                                 .to_broadcast([P, A_H, A_ROPE])))
                    if k == 6:
                        rope(proj[:, :, B_KC:B_KC + 128], 2, HD, 16, 8, ("heads", l, 2))
                        latents_out()
                        copy_windows(SECOND, l, 1)
                    if k == 7:
                        rope(proj[:, :, B_KS:B_KS + 128], 2, HD, 16, 8, ("heads", l, 4))

                def gates():
                    dve.wait_ge(small_act.sem, small_act.at(("gate", l)))
                    link(dve.tensor_scalar(gate[:, :], gate[:, :], 1.0, None, ALU.add))
                    link(dve.reciprocal(gate[:, :], gate[:, :]))

                def window_rope():
                    rope(proj[:, :, B_KW:B_KW + 128], 2, HD, 16, 8, ("heads", l, 12))

                def places_out():
                    dve.wait_ge(small_mm.sem, small_mm.at(("pe", l)))
                    link(dve.tensor_copy(pe_t[:, :], QT_B[SECOND.bank(("pe",))][:, 0:32]),
                         task_out_v, (l, "pe"))

                def blocks(w):
                    for sgn, pair in ((heads_out_a, 2 + 2 * (w > 0)), (heads_out_v, 3)):
                        dve.wait_ge(sgn.sem, sgn.at((l, True, pair)))
                    b4 = blk[w][:, :].rearrange("p (o g n) -> p g n o", o=16, g=B_G)
                    kc = kcv_t[:, 512 * w:512 * (w + 1)].rearrange("p (g s) -> p g s", g=B_G)
                    for q in range(2):
                        rows_ = slice(HD * q, HD * (q + 1))
                        for c in range(2):
                            seg = kc[rows_, :, 16 * c:16 * c + 240].rearrange("p g (n o l) -> p g n o l", o=8, l=2)
                            term = pe_t[rows_, 16 * w + 8 * c:16 * w + 8 * c + 8]
                            for g in range(B_G):
                                dve.tensor_tensor(
                                    b4[rows_, g, :, 8 * c:8 * c + 8], seg[:, g, :, :, q],
                                    term.unsqueeze(1).to_broadcast([HD, N_CMP, 8]), ALU.add)\
                                   .then_inc(prep_ready.sem, prep_ready.mark(("blk", l, w)))

                def compressed_out(w):
                    dve.wait_ge(small_mm.sem, small_mm.at(("cmp2", l, w)))
                    src = QT_B[SECOND.bank(("cmp2", w))]
                    if w == 0:
                        out = dve.tensor_copy(k_cmp[0:HD, :], src[0:HD, 0:30])
                    else:
                        out = dve.tensor_copy(v_cmp[0:N_CMP, :], src[0:N_CMP, 0:2 * HD])
                    link(out, task_out_v, (l, "cmp2", w))

                def diff_sums(c):
                    dve.wait_ge(task_out_a.sem, task_out_a.at((l, "back", c)))
                    lo = 4 * c - 8
                    link(dve.tensor_reduce(sumsq[:, lo:lo + 4],
                                           junk[:, 512:768].rearrange("p (i d) -> p i d", d=HD), AX.X, ALU.add),
                         head_squares, ("sub", l, c))

                def diff_norm(c):
                    dve.wait_ge(rstd_ready.sem, rstd_ready.at(("sub", l, c)))
                    v = diff_r[:, :].rearrange("p (i d) -> p i d", d=HD)
                    lo = 4 * c - 8
                    link(dve.tensor_tensor(v, v, rstd[:, lo:lo + 4].unsqueeze(2)
                                           .to_broadcast([P, 4, HD]), ALU.mult))
                    link(dve.tensor_tensor(v, v, small[:, A_QR + A_KVR:].unsqueeze(1)
                                           .to_broadcast([P, 4, HD]), ALU.mult), prep_ready, ("diff", l, c))

                def compressed_max():
                    dve.wait_ge(small_mm.sem, small_mm.at(("s_cmp", l)))
                    sc = s_cmp[:, 0:180].rearrange("p (h n) -> p h n", h=B_H)
                    link(dve.tensor_tensor(
                        sc, QT_B[SECOND.bank(("scores",))][:, 0:180].rearrange("p (h n) -> p h n", h=B_H),
                        cst[:, C_CM:C_CM + 30].unsqueeze(1).to_broadcast([P, B_H, 30]), ALU.add),
                        task_out_v, (l, "scores"))
                    link(dve.tensor_reduce(cmp_max[:, :], sn, AX.X, ALU.max, negate=True))
                    link(dve.tensor_tensor(sn, sn, cmp_max[:, :].unsqueeze(2).to_broadcast([P, 12, N_CMP]),
                                           ALU.add), prep_ready, ("s_cmp", l))

                def compressed_scale():
                    dve.wait_ge(small_act.sem, small_act.at(("s_cmp", l)))
                    link(dve.tensor_reduce(cmp_coef[:, :], sn, AX.X, ALU.add))
                    link(dve.reciprocal(cmp_coef[:, :], cmp_coef[:, :]))
                    c3v = cmp_coef[:, :].rearrange("p (h t) -> p h t", t=NT)
                    link(dve.tensor_tensor(c3v, c3v, cst[:, C_RV:C_RV + 2].unsqueeze(1)
                                           .to_broadcast([P, B_H, NT]), ALU.mult))
                    link(dve.tensor_tensor(c3v, c3v, gate4[:, :, :, 0].rearrange("p t h -> p h t"), ALU.mult))
                    link(dve.tensor_tensor(sn, sn, cmp_coef[:, :].unsqueeze(2)
                                           .to_broadcast([P, 12, N_CMP]), ALU.mult),
                         prep_ready, ("p_cmp", l))

                def compressed_probs(i):
                    dve.wait_ge(small_mm.sem, small_mm.at(("pc", l, i)))
                    link(dve.tensor_copy(pc_t[i % 2][:, :], QT_B[SECOND.bank(("pc", i))][:, 0:SEQ]),
                         task_out_v, (l, "pc", i))

                sn = s_cmp[:, 0:180].rearrange("p (i c) -> p i c", c=N_CMP)
                hooks = {0: [latent_keys, latent_rope, places_out], 1: [window_rope, gates], 4: [lambda: blocks(0)],
                         5: [lambda: blocks(1)], 
                         8: [lambda: diff_sums(6)], 9: [lambda: compressed_out(0)],
                         10: [lambda: compressed_out(1), lambda: diff_norm(6)],
                         11: [lambda: chunk_lo(("o2", l, 6), 6, QT_B[SECOND.bank(("forth", 6))])],
                         12: [lambda: diff_sums(7)], 13: [lambda: diff_norm(7)], 14: [compressed_max],
                         15: [compressed_scale],
                         16: [lambda: compressed_probs(0),
                              lambda: chunk_lo(("o2", l, 7), 7, QT_B[SECOND.bank(("forth", 7))])]}
                for i in range(1, B_H):
                    hooks[16 + 2 * i] = [lambda i=i: compressed_probs(i)]
                projection(u, 9, prepare)
                u += 9
                attend(SECOND, l, hooks)
                for k in range(4):
                    split_lo(u + k + AHEAD)
                    dve.wait_ge(unit_used, u + k + 1)
                    xs = x[:, :, 256 * k:256 * (k + 1)]
                    link(dve.tensor_tensor(xs, ACC[k][:, :].rearrange("p (t n) -> p t n", t=NT), xs, ALU.add),
                         prep_ready, ("rows", ("ffn2", l), k))
                u += 4
                turn_lo(("ffn2", l), 11 + 3 * l)
                ffn(3 + 2 * l)
                u += 3 * NG
                add_ffn(3 + 2 * l, "final" if l else ("ffn1", 1))
            n = norm_column(15)
            dve.wait_ge(rstd_ready.sem, rstd_ready.at(("norm", 15)))
            dve.wait_ge(gain_landed[0], 48)
            for t in range(NT):
                dve.scalar_tensor_tensor(h[:, t, :], x[:, t, :], rstd[:, n + t:n + t + 1], gain[0][:, :],
                                         ALU.mult, ALU.mult)\
                   .then_inc(rows_ready.sem, rows_ready.mark(("final", t)))

        @block.tensor
        def _(pe):
            def turn_piece(name, p, src=x, landed=None):
                if landed:
                    pe.wait_ge(landed, 16)
                else:
                    pe.wait_ge(prep_ready.sem, prep_ready.at(("rows", name, p)))
                if name == ("mix", 0):
                    pe.wait_ge(turned_lo.sem, turned_lo.at(("mem", p)))
                for e in range(2):
                    for t in range(NT):
                        c = 2 * p + e
                        last = pe.transpose(TURN[p][:, SEQ * e + P * t:SEQ * e + P * (t + 1)],
                                            src[:, t, P * c:P * (c + 1)], ident)
                last.then_inc(turned.sem, turned.mark((name, p)))

            def turn(name, src=x, landed=None):
                for p in range(4):
                    turn_piece(name, p, src, landed)

            def three(out, hi, lo, w_h, w_l, first, last):
                pe.matmul(out, hi, w_h, start=first, stop=False)
                pe.matmul(out, lo, w_h, start=False, stop=False)
                return pe.matmul(out, hi, w_l, start=False, stop=last)

            def projection(u0, n, k0, hi=xt_hi, lo=xt_lo, seq=0, chunks=None, pieces=None,
                           before=None):
                order = ORDER if chunks else range(KC)
                for k in range(n):
                    s = (u0 + k) % RING
                    if before and k in before:
                        before[k]()
                    pe.wait_ge(lo_ready, u0 + k + 1)
                    if seq + k >= 4:
                        pe.wait_ge(proj_out.sem, proj_out.at(("unit", u0 + k - 4)))
                    for t in range(NT):
                        for c in order:
                            if chunks and k == 0 and t == 0:
                                pe.wait_ge(turned_lo.sem, turned_lo.at((*chunks, c)))
                            if pieces and k == 0 and t == 0 and c % 2 == 0:
                                pe.wait_ge(turned_lo.sem, turned_lo.at((pieces, c // 2)))
                            last = three(ACC[(k0 + k) % 4][:, 256 * t:256 * (t + 1)],
                                         xt_chunk(t, c, hi[:, :]), xt_chunk(t, c, lo[:, :]),
                                         w_hi[s][:, 256 * c:256 * (c + 1)], w_lo[s][:, 256 * c:256 * (c + 1)],
                                         c == order[0], c == order[-1])
                    last.then_inc(unit_used, 1)

            def ffn(f, pieces):
                u0 = ffns[f][0]
                base = NG * f

                def wide(u, i, out, first=False):
                    s = u % RING
                    pe.wait_ge(lo_ready, u + 1 + 6 * i)
                    w = [v[s][:, :].rearrange("p (c n) -> p c n", c=KC) for v in (w_hi, w_lo)]
                    for m in range(2):
                        for c in range(KC):
                            if first and m == 0 and c % 2 == 0:
                                pe.wait_ge(turned_lo.sem, turned_lo.at((pieces, c // 2)))
                            o = out[:, SEQ * m:SEQ * (m + 1)]
                            sl = slice(SEQ * c, SEQ * (c + 1))
                            cols = slice(P * m, P * (m + 1))
                            pe.matmul(o, w[0][:, c, cols], xt_hi[:, sl], start=(c == 0), stop=False)
                            pe.matmul(o, w[0][:, c, cols], xt_lo[:, sl], start=False, stop=False)
                            last = pe.matmul(o, w[1][:, c, cols], xt_hi[:, sl], start=False,
                                             stop=(c == KC - 1))
                    return last

                def gate_up(u, i, g, p, used_before):
                    if used_before:
                        pe.wait_ge(hidden_ready, base + g - 1)
                    wide(u, i, G_B[p]).then_inc(unit_used, 1)
                    wide(u + 1, i, U_B[p]).then_inc(unit_used, 1)

                def down(u, i, g, p, first, last_group):
                    s = u % RING
                    pe.wait_ge(lo_ready, u + 1 + 6 * i)
                    pe.wait_ge(hidden_lo, base + g + 1)
                    for b in range(2):
                        for t in range(NT):
                            for m in range(2):
                                lo = SEQ * m + P * t
                                last = three(ACC[2 * t + b][:, :], hid_hi[p][:, lo:lo + P],
                                             hid_lo[p][:, lo:lo + P],
                                             w_hi[s][:, D * m + 512 * b:D * m + 512 * (b + 1)],
                                             w_lo[s][:, D * m + 512 * b:D * m + 512 * (b + 1)],
                                             first and m == 0, last_group and m == 1)
                        if last_group and b == 0:
                            last.then_inc(half_used, 1)
                    last.then_inc(unit_used, 1)

                wide(u0, 0, G_B[0], True).then_inc(unit_used, 1)
                wide(u0 + 1, 0, U_B[0]).then_inc(unit_used, 1)
                pe.wait_ge(prep_ready.sem, prep_ready.at(("diagonal", f)))
                pe.matmul(ACC[0][:, 0:SEQ], ones[:, :], rstd_diag, start=True, stop=True)\
                  .then_inc(small_mm.sem, small_mm.mark(("rstd rows", f)))
                gate_up(u0 + 2, 0, 1, 1, False)
                pe.wait_ge(prep_ready.sem, prep_ready.at(("rstd rows", f)))
                down(u0 + 4, 0, 0, 0, True, False)
                with pe.Fori(0, 4) as i:
                    for j in range(2):
                        gate_up(u0 + 5 + 3 * j, i, 2 * i + j + 2, j, True)
                        down(u0 + 7 + 3 * j, i, 2 * i + j + 1, 1 - j, False, False)
                gate_up(u0 + 29, 0, 10, 0, True)
                down(u0 + 31, 0, 9, 1, False, False)
                down(u0 + 32, 0, 10, 0, False, True)

            def bank_free(part, l, task):
                prev = part.before(task)
                if prev is None:
                    return
                if prev[0] == "windows":
                    sgn = (heads_out_a, heads_out_v)[prev[1] % 2]
                    pe.wait_ge(sgn.sem, sgn.at((l, part is SECOND, prev[1])))
                elif prev[0] == "cmp1":
                    if task[0] != "cmp1":
                        pe.wait_ge(small_act.sem, small_act.at(("cmp", l)))
                elif prev[0] == "back":
                    pe.wait_ge(task_out_a.sem, task_out_a.at((l, *prev)))
                elif prev[0] == "forth":
                    pe.wait_ge(turned_lo.sem, turned_lo.at(("o2", l, prev[1])))
                else:
                    pe.wait_ge(task_out_v.sem, task_out_v.at((l, *prev)))

            def turn_windows(part, l, p, ready=()):
                bank_free(part, l, ("windows", p))
                for sgn, key in ready:
                    pe.wait_ge(sgn.sem, sgn.at(key))
                for m, w in enumerate(part.pairs[p]):
                    for t in range(NT):
                        last = pe.transpose(QT_B[part.bank(("windows", p))]
                                            [0:w.width, SEQ * m + P * t:SEQ * m + P * (t + 1)],
                                            token_rows(w.src, t, w.col, w.width), ident)
                last.then_inc(heads_turned.sem, heads_turned.mark((l, part is SECOND, p)))

            def attend(part, l, task_of, ready={}, values_from={}):
                second = part is SECOND
                N = len(part.units)

                def scores(n):
                    unit = part.units[n]
                    if n >= 2:
                        pe.wait_ge(probs_ready.sem, probs_ready.at((l, second, n - 2)))
                    for odd, p in part.pairs_for(n, part.step_of).items():
                        if p is not None:
                            sgn = (heads_out_a, heads_out_v)[odd]
                            pe.wait_ge(sgn.sem, sgn.at((l, second, p)))
                    for t in range(NT):
                        lo, width = scores_at(unit.kind, t)
                        masks = {b: m for b, m in MASKED[unit.kind].items() if BLOCKS[unit.kind][b][0] == t}
                        last = pe.matmul(S_B[n % 2][:, lo:lo + width],
                                         slot(unit.q, 0, unit.rows, P * t, P * (t + 1)),
                                         slot(unit.k, 0, unit.rows, 0, width), start=True, stop=not masks)
                        for b, m in masks.items():
                            last = pe.matmul(S_B[n % 2][:, P * b:P * (b + 1)], ident_b[:, :],
                                             (up_b if m == "upper" else lo_b)[:, :], start=False, stop=True)
                    last.then_inc(scores_ready.sem, scores_ready.mark((l, second, n)))

                def turn_probs(n):
                    kind = part.units[n].kind
                    pe.wait_ge(probs_scaled.sem, probs_scaled.at((l, second, n)))
                    if n >= 2:
                        sgn = probs_out_a if out_by_scalar(second, n - 2) else probs_out_v
                        pe.wait_ge(sgn.sem, sgn.at((l, second, n - 2)))
                    for b in range(len(BLOCKS[kind])):
                        to = TURNED_AT[kind][b]
                        last = pe.transpose(PT_B[n % 2][:, to:to + P], probs[n % 3][:, P * b:P * (b + 1)],
                                            ident)
                    last.then_inc(probs_turned.sem, probs_turned.mark((l, second, n)))

                def values(n):
                    unit = part.units[n]
                    src, col = unit.value
                    k = ORDER.index(unit.chunk)
                    o = O_B[k % 2][HD * unit.half:HD * (unit.half + 1), :]
                    if k >= 2:
                        c = ORDER[k - 2]
                        if second and c >= 6:
                            pe.wait_ge(task_out_a.sem, task_out_a.at((l, "diff", c)))
                        else:
                            pe.wait_ge(turned_lo.sem, turned_lo.at((OUT[second], l, c)))
                    for sgn, key in values_from.get(n, ()):
                        pe.wait_ge(sgn.sem, sgn.at(key))
                    if unit.factor and unit.factor[0:1] + unit.factor[2:] == ("gate", 1):
                        i = unit.factor[1]
                        pe.wait_ge(task_out_v.sem, task_out_v.at((l, "pc", i)))
                        g = i // (B_H // B_G)
                        pe.matmul(o[:, 0:SEQ], v_cmp[:, HD * g:HD * (g + 1)], pc_t[i % 2][:, :],
                                  start=True, stop=False)
                    sgn = probs_out_a if out_by_scalar(second, n) else probs_out_v
                    pe.wait_ge(sgn.sem, sgn.at((l, second, n)))
                    pt = probs_t[n % 2]
                    pe.matmul(o[:, 0:SEQ], token_rows(src, 0, col, HD), pt[:, 0:SEQ],
                              start=unit.opens, stop=False)
                    if unit.kind == CAUSAL:
                        last = pe.matmul(o[:, P:SEQ], token_rows(src, 1, col, HD), pt[:, SEQ:SEQ + P],
                                         start=False, stop=unit.closes)
                    else:
                        last = pe.matmul(o[:, 0:SEQ], token_rows(src, 1, col, HD), pt[:, SEQ:2 * SEQ],
                                         start=False, stop=unit.closes)
                    last.then_inc(values_ready.sem, values_ready.mark((l, second, n)))

                scores(0)
                for n in range(N + 3):
                    if n + 1 < N:
                        scores(n + 1)
                    if 0 <= n - 2 < N:
                        turn_probs(n - 2)
                    if n >= 3:
                        values(n - 3)
                    for task in part.tasks.get(n, []):
                        if task[0] == "windows":
                            turn_windows(part, l, task[1], ready.get(task[1], ()))
                        else:
                            task_of(task)

            pe.wait_ge(consts_landed, 32)
            pe.wait_ge(rows_landed, 16 * len(gain_rows))
            pe.transpose(ACC[3][:, 0:88], proj_at[0:88, 512:640], ident[0:88, 0:88])\
              .then_inc(small_mm.sem, small_mm.mark("gains_t"))
            turn("mem", h, mem_landed)
            pe.wait_ge(prep_ready.sem, prep_ready.at("gains_t"))
            pe.wait_ge(pool_order.sem, pool_order.at("ones"))
            u = 0
            for l in range(2):
                if l:
                    pe.wait_ge(prep_ready.sem, prep_ready.at(("fsum", l - 1)))
                projection(u, 2, 2, mem_hi, mem_lo, pieces="mem" if l == 0 else None,
                           before={1: lambda: turn(("mix", l), x, None if l else x_landed)})
                part = (FIRST0, FIRST1)[l]
                if l == 0:
                    pe.wait_ge(prep_ready.sem, prep_ready.at("consts"))

                def memory_windows():
                    turn_windows(part, l, 0, [(proj_out, ("unit", u + 4))])
                    turn_windows(part, l, 1, [(proj_out, ("unit", u + 5))])
                projection(u + 2, 6, 4, seq=2, pieces=("mix", l), before={5: memory_windows})
                u += 8
                attend(part, l, None,
                       {2: [(prep_ready, ("piece", l, 3))], 5: [(prep_ready, ("piece", l, 4))]},
                       {0: [(proj_out, ("unit", u - 1))]})
                projection(u, 4, 0, chunks=("o", l))
                u += 4
                turn(("ffn", l))
                ffn(l, ("ffn", l))
                u += 3 * NG
            for l in range(2):
                turn(("ffn1", l))
                ffn(2 + 2 * l, ("ffn1", l))
                u += 3 * NG
                turn(("mix2", l))

                def latents():
                    pe.wait_ge(prep_ready.sem, prep_ready.at(("latent", l)))
                    for t in range(NT):
                        pe.transpose(bank[2][:, P * t:P * (t + 1)], proj[:, t, 0:P], ident)
                        pe.transpose(bank[2][0:HD, 256 + P * t:256 + P * (t + 1)], proj[:, t, P:A_QR], ident)
                        last = pe.transpose(bank[3][:, P * t:P * (t + 1)], proj[:, t, A_QR:A_QR + A_KVR], ident)
                    last.then_inc(small_mm.sem, small_mm.mark(("latent", l)))

                def latent_queries():
                    pe.wait_ge(prep_ready.sem, prep_ready.at(("lat_t", l)))
                    pe.wait_ge(layer_landed, 160 * (l + 1))
                    for t in range(NT):
                        for b in range(2):
                            o = bank[2 * t + b][:, 0:288]
                            pe.matmul(o, lat_t[:, P * t:P * (t + 1)], uq[:, 288 * b:288 * (b + 1)],
                                      start=True, stop=False)
                            pe.matmul(o, lat_t[0:HD, 256 + P * t:256 + P * (t + 1)],
                                      uq[0:HD, 576 + 288 * b:576 + 288 * (b + 1)], start=False, stop=True)\
                              .then_inc(small_mm.sem, small_mm.mark(("uq", l, t, b)))
                    turn_windows(SECOND, l, 0, [(prep_ready, ("heads", l, 0)), (proj_out, ("unit", u + 5))])
                    turn_windows(SECOND, l, 1, [(proj_out, ("unit", u + 6))])

                def latent_keys():
                    pe.wait_ge(small_act.sem, small_act.at(("uq", l)))
                    for t in range(NT):
                        for b in range(2):
                            pe.matmul(bank[2 * t + b][:, 0:384], lat_t[:, 512 + P * t:512 + P * (t + 1)],
                                      ukv[:, 384 * b:384 * (b + 1)], start=True, stop=True)\
                              .then_inc(small_mm.sem, small_mm.mark(("ukv", l, t, b)))
                    pe.wait_ge(small_act.sem, small_act.at(("ukv", l)))

                def task_of(task):
                    bank_free(SECOND, l, task)
                    out = QT_B[SECOND.bank(task)]
                    name, which = task[0], task[-1]
                    if name == "pe":
                        pe.wait_ge(phi_landed, 96 * (l + 1))
                        for w in range(2):
                            last = pe.transpose(out[:, 16 * w:16 * (w + 1)], pe_rows[0:16, P * w:P * (w + 1)],
                                                ident[0:16, 0:16])
                        last.then_inc(small_mm.sem, small_mm.mark(("pe", l)))
                    elif name == "cmp1":
                        pe.wait_ge(prep_ready.sem, prep_ready.at(("blk", l, which)))
                        for o in range(16):
                            last = pe.matmul(out[0:HD, 32 * which:32 * which + 30], phi1[which][:, HD * o:HD * (o + 1)],
                                             blk[which][:, 30 * o:30 * (o + 1)], start=(o == 0), stop=(o == 15))
                        last.then_inc(small_mm.sem, small_mm.mark(("cmp1", l, which)))
                    elif name == "cmp2":
                        pe.wait_ge(small_act.sem, small_act.at(("cmp", l)))
                        if which == 0:
                            last = pe.matmul(out[0:HD, 0:30], phi2[0:HD, 0:HD], hid_c[0][0:HD, :],
                                             start=True, stop=True)
                        else:
                            for g in range(B_G):
                                last = pe.matmul(out[0:N_CMP, HD * g:HD * (g + 1)],
                                                 hid_c[1][0:HD, N_CMP * g:N_CMP * (g + 1)],
                                                 phi2[0:HD, HD:2 * HD], start=True, stop=True)
                        last.then_inc(small_mm.sem, small_mm.mark(("cmp2", l, which)))
                    elif name == "back":
                        pe.wait_ge(task_out_a.sem, task_out_a.at((l, "diff", which)))
                        for t in range(NT):
                            last = pe.transpose(out[:, P * t:P * (t + 1)], diff_t[:, P * t:P * (t + 1)], ident)
                        last.then_inc(small_mm.sem, small_mm.mark(("back", l, which)))
                    elif name == "forth":
                        pe.wait_ge(prep_ready.sem, prep_ready.at(("diff", l, which)))
                        for t in range(NT):
                            last = pe.transpose(out[:, P * t:P * (t + 1)], diff_r[:, P * t:P * (t + 1)], ident)
                        last.then_inc(small_mm.sem, small_mm.mark(("forth", l, which)))
                    elif name == "scores":
                        pe.wait_ge(task_out_v.sem, task_out_v.at((l, "cmp2", 1)))
                        for sgn in (heads_out_a, heads_out_v):
                            pe.wait_ge(sgn.sem, sgn.at((l, True, 14 + (sgn is heads_out_v))))
                        for i in range(B_H):
                            g = i // (B_H // B_G)
                            q = SECOND.units[SPARSE0 + 2 * i].q
                            for t in range(NT):
                                last = pe.matmul(out[:, 30 * i + N_CMP * t:30 * i + N_CMP * (t + 1)],
                                                 slot(q, 0, P, P * t, P * (t + 1)),
                                                 k_cmp[:, N_CMP * g:N_CMP * (g + 1)], start=True, stop=True)
                        last.then_inc(small_mm.sem, small_mm.mark(("s_cmp", l)))
                    else:
                        pe.wait_ge(prep_ready.sem, prep_ready.at(("p_cmp", l)))
                        for t in range(NT):
                            lo = 30 * which + N_CMP * t
                            last = pe.transpose(out[:, P * t:P * (t + 1)], s_cmp[:, lo:lo + P], ident)
                        last.then_inc(small_mm.sem, small_mm.mark(("pc", l, which)))

                projection(u, 9, 1, pieces=("mix2", l), before={7: latents, 8: latent_queries})
                u += 9
                latent_keys()
                attend(SECOND, l, task_of,
                       {2: [(prep_ready, ("heads", l, 2)), (proj_out, ("unit", u - 1))],
                        4: [(prep_ready, ("heads", l, 4))],
                        5: [(prep_ready, ("latent heads", l))], 11: [(prep_ready, ("heads", l, 12))]})
                projection(u, 4, 0, chunks=("o2", l),
                           before={k: lambda k=k: turn_piece(("ffn2", l), k - 2) for k in (2, 3)})
                u += 4
                for p in (2, 3):
                    turn_piece(("ffn2", l), p)
                ffn(3 + 2 * l, ("ffn2", l))
                u += 3 * NG


def kernel(**inputs):
    import numpy as _np
    import concourse.bacc as _bacc
    from concourse import mybir as _mybir
    from concourse.bass_utils import run_bass_kernel_spmd as _run

    def program(noted):
        nc = _bacc.Bacc("TRN2", target_bir_lowering=False, num_devices=1)
        arrays, tensors = {}, {}
        for name, value in [*inputs.items(), ("constants", constants())]:
            v = _np.ascontiguousarray(value)
            arrays[f"in_{name}"] = v
            tensors[name] = nc.dram_tensor(f"in_{name}", v.shape, _mybir.dt.from_np(v.dtype),
                                           kind="ExternalInput").ap()
        tensors["out"] = nc.dram_tensor("out_x", (1, SEQ, D), F32, kind="ExternalOutput").ap()
        build(nc, tensors, noted)
        return nc, arrays

    noted = {}
    program(noted)
    nc, arrays = program(noted)
    r = _run(nc, [arrays], core_ids=[0])
    return r.results[0]["out_x"]
```
